# Optimizing a Trainium2 kernel written in Bass

```python
import math
import jax, jax.numpy as jnp
from jax import lax
import numpy as np

D_MODEL = 1024
BATCH = 1
SEQ = 512
DEPTH = 1

DIFF_HEADS = 4
DIFF_QK_DIM = 64
DIFF_V_DIM = 2 * DIFF_QK_DIM
DIFF_WIDTH = DIFF_HEADS * DIFF_V_DIM
MOBA_HEADS = 8
MOBA_HEAD_DIM = 64
MOBA_WIDTH = MOBA_HEADS * MOBA_HEAD_DIM
MOBA_BLOCK = 256
MOBA_TOPK = 3
MOBA_Q_CHUNK = 16
MIX_WIDTH = DIFF_WIDTH + MOBA_WIDTH
IN_WIDTH = 4 * DIFF_WIDTH + 4 * MOBA_WIDTH
N_BUCKETS = 32
MAX_DISTANCE = 128
N_BIAS_HEADS = DIFF_HEADS + MOBA_HEADS
Q_BLOCK = 128
NORM_EPS = 1e-6
SUBLN_EPS = 1e-5
NEG = -1e30

kernel_name = "hymba_diff_moba_hybrid"

def rmsnorm(x, g, eps=NORM_EPS):
    xf = x.astype(jnp.float32)
    ms = jnp.mean(xf * xf, axis=-1, keepdims=True)
    return (xf * lax.rsqrt(ms + eps) * g.astype(jnp.float32)).astype(x.dtype)

def rel_bucket(dist):
    n = jnp.maximum(dist, 0)
    max_exact = N_BUCKETS // 2
    nf = jnp.maximum(n, 1).astype(jnp.float32)
    large = max_exact + (jnp.log(nf / max_exact) / math.log(MAX_DISTANCE / max_exact)
                         * (N_BUCKETS - max_exact)).astype(jnp.int32)
    large = jnp.minimum(large, N_BUCKETS - 1)
    return jnp.where(n < max_exact, n, large)

def diff_attention(q, k, v, lam, lambda_init, subln_g, bias_tab):
    B, H, S = q.shape[0], q.shape[1], q.shape[2]
    scale = DIFF_QK_DIM ** -0.5
    nqb = S // Q_BLOCK
    q_blocks = jnp.moveaxis(q.reshape(B, H, nqb, Q_BLOCK, 2, DIFF_QK_DIM), 2, 0)
    k_pos = jnp.arange(S)

    def one_block(args):
        qb, blk = args
        q_pos = blk * Q_BLOCK + jnp.arange(Q_BLOCK)
        dist = q_pos[:, None] - k_pos[None, :]
        bias = jnp.moveaxis(bias_tab[rel_bucket(dist)], -1, 0)
        logits = jnp.einsum('bhqcd,bhkcd->bhcqk', qb, k).astype(jnp.float32) * scale
        logits = logits + bias[None, :, None].astype(jnp.float32)
        logits = jnp.where(dist >= 0, logits, -jnp.inf)
        p = jax.nn.softmax(logits, axis=-1)
        w = p[:, :, 0] - lam * p[:, :, 1]
        return jnp.einsum('bhqk,bhkd->bhqd', w.astype(v.dtype), v)

    out = lax.map(one_block, (q_blocks, jnp.arange(nqb)))
    out = jnp.moveaxis(out, 0, 2).reshape(B, H, S, DIFF_V_DIM)
    return rmsnorm(out, subln_g, SUBLN_EPS) * (1.0 - lambda_init)

def moba_attention(q, k, v, bias_tab):
    B, H, S, D = q.shape
    scale = D ** -0.5
    nb = -(-S // MOBA_BLOCK)
    pad = nb * MOBA_BLOCK - S
    kp = jnp.pad(k, ((0, 0), (0, 0), (0, pad), (0, 0)))
    vp = jnp.pad(v, ((0, 0), (0, 0), (0, pad), (0, 0)))
    kb = kp.reshape(B, H, nb, MOBA_BLOCK, D)
    vb = vp.reshape(B, H, nb, MOBA_BLOCK, D)
    k_mean = jnp.mean(kb.astype(jnp.float32), axis=3)
    top = max(1, min(MOBA_TOPK, nb - 1))
    bias_flat = bias_tab.T.reshape(-1)
    head_off = (jnp.arange(H) * N_BUCKETS)[None, :, None, None, None]
    nc = S // MOBA_Q_CHUNK
    q_chunks = jnp.moveaxis(q.reshape(B, H, nc, MOBA_Q_CHUNK, D), 2, 0)
    gather_blocks = jax.vmap(jax.vmap(lambda blocks, idx: blocks[idx]))
    blk_off = jnp.arange(MOBA_BLOCK)

    def one_chunk(args):
        qb, ci = args
        t0 = ci * MOBA_Q_CHUNK
        q_pos = t0 + jnp.arange(MOBA_Q_CHUNK)
        cur = t0 // MOBA_BLOCK
        gate = jnp.einsum('bhqd,bhnd->bhqn', qb.astype(jnp.float32), k_mean)
        gate = jnp.where(jnp.arange(nb) < cur, gate, NEG)
        _, idx = lax.top_k(gate, top)
        valid = idx < cur
        k_sel = gather_blocks(kb, idx)
        v_sel = gather_blocks(vb, idx)
        k_sel_pos = idx[..., None] * MOBA_BLOCK + blk_off
        s_sel = jnp.einsum('bhqd,bhqtkd->bhqtk', qb, k_sel).astype(jnp.float32) * scale
        dist_sel = q_pos[:, None, None] - k_sel_pos
        s_sel = s_sel + bias_flat[head_off + rel_bucket(dist_sel)].astype(jnp.float32)
        s_sel = jnp.where(valid[..., None], s_sel, -jnp.inf)
        s_sel = s_sel.reshape(B, H, MOBA_Q_CHUNK, top * MOBA_BLOCK)
        k_own = lax.dynamic_slice_in_dim(kb, cur, 1, axis=2)[:, :, 0]
        v_own = lax.dynamic_slice_in_dim(vb, cur, 1, axis=2)[:, :, 0]
        dist_own = q_pos[:, None] - (cur * MOBA_BLOCK + blk_off)[None, :]
        bias_own = jnp.moveaxis(bias_tab[rel_bucket(dist_own)], -1, 0)
        s_own = jnp.einsum('bhqd,bhkd->bhqk', qb, k_own).astype(jnp.float32) * scale
        s_own = s_own + bias_own[None].astype(jnp.float32)
        s_own = jnp.where(dist_own >= 0, s_own, -jnp.inf)
        p = jax.nn.softmax(jnp.concatenate([s_sel, s_own], axis=-1), axis=-1)
        p_sel = p[..., :top * MOBA_BLOCK].reshape(B, H, MOBA_Q_CHUNK, top, MOBA_BLOCK)
        p_own = p[..., top * MOBA_BLOCK:]
        return (jnp.einsum('bhqtk,bhqtkd->bhqd', p_sel.astype(v.dtype), v_sel)
                + jnp.einsum('bhqk,bhkd->bhqd', p_own.astype(v.dtype), v_own))

    out = lax.map(one_chunk, (q_chunks, jnp.arange(nc)))
    return jnp.moveaxis(out, 0, 2).reshape(B, H, S, D)

def setup_inputs(seed: int = 0) -> dict:
    key = jax.random.key(seed)
    ks = jax.random.split(key, 8)
    x = jax.random.normal(ks[0], (BATCH, SEQ, D_MODEL), jnp.float32)
    norm_pre_g = 1.0 + 0.02 * jax.random.normal(ks[1], (DEPTH, D_MODEL), jnp.float32)
    w_in = jax.random.normal(ks[2], (DEPTH, D_MODEL, IN_WIDTH), jnp.float32) * D_MODEL ** -0.5
    diff_lambda = 0.1 * jax.random.normal(ks[3], (DEPTH, 4, DIFF_QK_DIM), jnp.float32)
    diff_subln_g = 1.0 + 0.02 * jax.random.normal(ks[4], (DEPTH, DIFF_V_DIM), jnp.float32)
    w_out = jax.random.normal(ks[5], (DEPTH, MIX_WIDTH, D_MODEL), jnp.float32) * MIX_WIDTH ** -0.5
    norm_post_g = 1.0 + 0.02 * jax.random.normal(ks[6], (DEPTH, D_MODEL), jnp.float32)
    rel_bias = 0.2 * jax.random.normal(ks[7], (N_BUCKETS, N_BIAS_HEADS), jnp.float32)
    return {"x": x, "norm_pre_g": norm_pre_g, "w_in": w_in, "diff_lambda": diff_lambda,
            "diff_subln_g": diff_subln_g, "w_out": w_out, "norm_post_g": norm_post_g,
            "rel_bias": rel_bias}

def reference(x, norm_pre_g, w_in, diff_lambda, diff_subln_g, w_out, norm_post_g, rel_bias):
    B, S, _ = x.shape
    splits = [DIFF_WIDTH, 2 * DIFF_WIDTH, 3 * DIFF_WIDTH, 4 * DIFF_WIDTH,
              4 * DIFF_WIDTH + MOBA_WIDTH, 4 * DIFF_WIDTH + 2 * MOBA_WIDTH,
              4 * DIFF_WIDTH + 3 * MOBA_WIDTH]
    bias_diff = rel_bias[:, :DIFF_HEADS]
    bias_moba = rel_bias[:, DIFF_HEADS:]
    for layer in range(DEPTH):
        h = rmsnorm(x, norm_pre_g[layer])
        u = jnp.einsum('bsd,de->bse', h, w_in[layer])
        dq, dk, dv, dg, mq, mk, mv, mg = jnp.split(u, splits, axis=-1)
        lambda_init = 0.8 - 0.6 * math.exp(-0.3 * layer)
        lp = diff_lambda[layer].astype(jnp.float32)
        lam = jnp.exp(jnp.sum(lp[0] * lp[1])) - jnp.exp(jnp.sum(lp[2] * lp[3])) + lambda_init
        to_qk = lambda t: jnp.transpose(t.reshape(B, S, DIFF_HEADS, 2, DIFF_QK_DIM), (0, 2, 1, 3, 4))
        dvh = jnp.transpose(dv.reshape(B, S, DIFF_HEADS, DIFF_V_DIM), (0, 2, 1, 3))
        a_out = diff_attention(to_qk(dq), to_qk(dk), dvh, lam, lambda_init,
                               diff_subln_g[layer], bias_diff)
        a_out = jnp.transpose(a_out, (0, 2, 1, 3)).reshape(B, S, DIFF_WIDTH) * jax.nn.silu(dg)
        to_h = lambda t: jnp.transpose(t.reshape(B, S, MOBA_HEADS, MOBA_HEAD_DIM), (0, 2, 1, 3))
        b_out = moba_attention(to_h(mq), to_h(mk), to_h(mv), bias_moba)
        b_out = jnp.transpose(b_out, (0, 2, 1, 3)).reshape(B, S, MOBA_WIDTH) * jax.nn.silu(mg)
        y = jnp.einsum('bse,ed->bsd', jnp.concatenate([a_out, b_out], axis=-1), w_out[layer])
        x = x + rmsnorm(y, norm_post_g[layer])
    return x


_drawn_inputs = setup_inputs


def setup_inputs(seed=0):
    import zlib

    import numpy as np

    out = dict(_drawn_inputs(seed))
    spreads = {}
    factors = {'diff_lambda': 8.0, 'diff_subln_g': 4.119, 'norm_post_g': 3.88}
    for name, (base, spread) in spreads.items():
        noise = np.random.default_rng([zlib.crc32(name.encode()), seed]).standard_normal(out[name].shape)
        drawn = base * np.exp(spread * noise) if base else spread * noise
        out[name] = __import__('jax').numpy.asarray(drawn.astype(out[name].dtype))
    for name, factor in factors.items():
        out[name] = (out[name] * factor).astype(out[name].dtype)
    return out
```

```python
import math
from contextlib import ExitStack

import concourse.bass as bass
from concourse import mybir


def bass_hymba_diff_moba_layer(
    nc: bass.Bass,
    x: bass.AP,
    norm_pre_g: bass.AP,
    w_in: bass.AP,
    diff_lambda: bass.AP,
    diff_subln_g: bass.AP,
    w_out: bass.AP,
    norm_post_g: bass.AP,
    rel_bias: bass.AP,
    out: bass.AP,
):
    fp32 = mybir.dt.float32
    fp16 = mybir.dt.float16
    ALU = mybir.AluOpType
    ACT = mybir.ActivationFunctionType

    P = 128
    SEQ, DM = x.shape[1], x.shape[2]
    TILES = SEQ // P
    KT = DM // P
    WIDTH = SEQ
    DH = 64
    CHUNKS = WIDTH // P
    DIFF_HEADS = 4
    HEADS = rel_bias.shape[1]
    BUCKETS = rel_bias.shape[0]
    MAX_DISTANCE = 128
    NORM_EPS, SUBLN_EPS = 1e-6, 1e-5
    LAMBDA_INIT = 0.8 - 0.6 * math.exp(-0.3 * 0)
    MASKED = -3e38

    W_SCALE = 64.0
    Q_SCALE = DH ** -0.5 / W_SCALE
    U_SCALE = 1.0 / W_SCALE
    GATE_SCALE = 2.0 * W_SCALE

    D = WIDTH
    GROUPS = [("v", 0, 2 * D), ("q", 0, 0), ("k", 0, D), ("g", 0, 3 * D),
              ("v", 1, 6 * D), ("k", 1, 5 * D), ("q", 1, 4 * D), ("g", 1, 7 * D)]
    IN_UNITS = len(GROUPS) * TILES
    Y_UNITS = 2 * TILES
    UNITS = IN_UNITS + Y_UNITS
    QUARTERS = 4 * (len(GROUPS) + 2)
    DOWN = list(range(TILES - 1, -1, -1))

    def unit_of(u):
        if u >= IN_UNITS:
            y = u - IN_UNITS
            return "y", y % 2, DOWN[y // 2], len(GROUPS) + y % 2
        kind, region, _ = GROUPS[u // TILES]
        i = u % TILES
        return kind, region, DOWN[i] if kind == "g" else i, u // TILES

    UNIT = {unit_of(u)[:3]: u for u in range(UNITS)}

    STEPS = [(r, t, c) for r in range(2) for t in DOWN for c in range(CHUNKS)]
    NSTEP = len(STEPS)
    SLOTS = NSTEP + 2
    HALF = NSTEP // 2
    FILL = []
    for j in range(SLOTS):
        if j < HALF:
            u = 3 * TILES + j
            FILL.append(([(u, 0), (u, 1)], [(u, 2), (u, 3)]))
        elif j < NSTEP:
            u, q = 3 * TILES + HALF + (j - HALF) // 2, 2 * (j % 2)
            FILL.append(([(u, q)], [(u, q + 1)]))
        else:
            u = 3 * TILES + HALF + HALF // 2 + j - NSTEP
            FILL.append(([(u, 0), (u, 1)], [(u, 2), (u, 3)]))
    FILL_END = [[u for part in FILL[j] for u, q in part if q == 3] for j in range(SLOTS)]
    LAST_UNITS = list(range(UNITS - 2, UNITS))
    SPLIT_AHEAD = 4
    SPLIT_IN_SLOT = [[3 * TILES + SPLIT_AHEAD + j] if 3 * TILES + SPLIT_AHEAD + j < QUARTERS else []
                     for j in range(SLOTS)]
    AT_SLOT = {DOWN[i]: HALF + 4 * (i + 1) + 3 for i in range(TILES - 1)}
    AT_SLOT[0] = SLOTS - 1
    POST_SLOT = {STEPS[i][:2]: i + 2 for i in range(NSTEP) if i % 4 == 3}

    PT_ORDER = [("x", 0), ("x", 2)]
    for j in range(SLOTS):
        if 1 <= j <= NSTEP:
            PT_ORDER.append(("p", j - 1))
        PT_ORDER += [("a", t) for t in DOWN if AT_SLOT[t] == j]
    PT_USE = {k: n for n, k in enumerate(PT_ORDER)}
    X_USES = 2

    def pt_use(*key):
        return PT_USE[key] - X_USES

    x_v = x[0].rearrange("(t p) d -> t p d", p=P)
    out_v = out[0].rearrange("(t p) d -> t p d", p=P)
    w_in_v = w_in[0].rearrange("(k p) n -> p k n", p=P)
    w_out_v = w_out[0].rearrange("(k p) n -> p k n", p=P)

    ROW = SEQ + P
    bias_rows = nc.dram_tensor("bias_rows", (HEADS, ROW), fp32, kind="Internal")
    strip_view = bass.AP(tensor=bias_rows, offset=0, ap=[[1, P], [ROW, HEADS], [1, SEQ]])

    def first_distance(b):
        exact = BUCKETS // 2
        if b <= exact:
            return b
        return next(n for n in range(exact, SEQ + 1)
                    if n == SEQ or min(exact + int(math.log(n / exact) / math.log(MAX_DISTANCE / exact)
                                                   * (BUCKETS - exact)), BUCKETS - 1) >= b)

    ctx = ExitStack()
    with ctx:
        def sb(name, shape, dt=fp32):
            return ctx.enter_context(nc.sbuf_tensor(name, shape, dt))

        def sem(name):
            return ctx.enter_context(nc.semaphore(name))

        arena = sb("arena", [P, 4 * DM])
        x_sb = arena[:, :].rearrange("p (t d) -> p t d", t=TILES)
        neglog = arena[:, 0:2 * DM].rearrange("p (b m n) -> p b m n", b=2, m=2)
        probs = arena[:, 2 * DM:4 * DM].rearrange("p (b m n) -> p b m n", b=2, m=2)
        area = sb("area", [P, 4 * DM])
        ht = area[:, :].bitcast(fp16).rearrange("p (h k s) -> p h k s", h=2, k=KT)
        at = area[:, 0:2 * DM].bitcast(fp16).rearrange("p (b h e s) -> p b h e s", b=2, h=2, e=KT)
        y_sb = area[:, 2 * DM:4 * DM].rearrange("p (b d) -> p b d", b=2)
        stage = sb("stage", [P, 4, 2 * WIDTH])
        w_hi = sb("w_hi", [P, 3, KT, WIDTH], fp16)
        w_lo = sb("w_lo", [P, 3, KT, WIDTH], fp16)
        q_hi = sb("q_hi", [P, 2 * CHUNKS, SEQ], fp16)
        q_lo = sb("q_lo", [P, 2 * CHUNKS, SEQ], fp16)
        k_hi = sb("k_hi", [P, 2 * CHUNKS, SEQ], fp16)
        k_lo = sb("k_lo", [P, 2 * CHUNKS, SEQ], fp16)
        v_hi = sb("v_hi", [P, TILES, 2 * WIDTH], fp16)
        v_lo = sb("v_lo", [P, TILES, 2 * WIDTH], fp16)
        gates = sb("gates", [P, 2, TILES, WIDTH])
        strips = sb("strips", [P, HEADS, SEQ])
        pt_hi = sb("pt_hi", [P, 2, 2, SEQ], fp16)
        pt_lo = sb("pt_lo", [P, 2, 2, SEQ], fp16)
        g_row = sb("g_row", [P, DM])
        subln = sb("subln", [P, 2 * DH])
        tanh_sb = sb("tanh_sb", [P, 2, WIDTH])
        heads_out = sb("heads_out", [P, WIDTH])
        junk = sb("junk", [P, DM], fp16)
        ident = sb("ident", [P, P])
        negmax = sb("negmax", [P, NSTEP, 2])
        sums = sb("sums", [P, NSTEP, 2])
        rsums = sb("rsums", [P, NSTEP, 2])
        ratio = sb("ratio", [P, HALF])
        lam_in = sb("lam_in", [P, 4, DH])
        lam_junk = sb("lam_junk", [P, 2, DH])
        lam_dot = sb("lam_dot", [P, 2])
        lam_exp = sb("lam_exp", [P, 2])
        neglam = sb("neglam", [P, 1])
        minus_half = sb("minus_half", [P, 4])
        x_sq = sb("x_sq", [P, TILES])
        x_ms = sb("x_ms", [P, TILES])
        x_rstd = sb("x_rstd", [P, TILES])
        sub_sq = sb("sub_sq", [P, TILES, DIFF_HEADS])
        sub_ms = sb("sub_ms", [P, TILES, DIFF_HEADS])
        sub_rstd = sb("sub_rstd", [P, TILES, DIFF_HEADS])
        y_sq = sb("y_sq", [P, TILES, 2])
        y_sum = sb("y_sum", [P, TILES])
        y_ms = sb("y_ms", [P, TILES])
        y_rstd = sb("y_rstd", [P, TILES])
        row_sb = tanh_sb[0:HEADS, :, :].rearrange("p b n -> p (b n)")[:, 0:ROW]
        rel_t = tanh_sb[0:HEADS, :, :].rearrange("p b n -> p (b n)")[:, ROW:ROW + BUCKETS]

        unit_ps = ctx.enter_context(nc.psum_tensor("unit_ps", [P, 2, 512], fp32))
        score_ps = ctx.enter_context(nc.psum_tensor("score_ps", [P, 2, 512], fp32))
        pt_ps = ctx.enter_context(nc.psum_tensor("pt_ps", [P, 2, 512], fp32))
        o_ps = ctx.enter_context(nc.psum_tensor("o_ps", [P, 2, 512], fp32))
        xt_banks = [pt_ps, score_ps]

        x_loaded = [sem(f"x_loaded{t}") for t in range(TILES)]
        gpre_loaded = sem("gpre_loaded")
        gpost_loaded = sem("gpost_loaded")
        small_loaded = sem("small_loaded")
        rel_loaded = sem("rel_loaded")
        rows_stored = sem("rows_stored")
        strips_loaded = sem("strips_loaded")
        w_loaded = [sem(f"w_loaded{i}") for i in range(4)]
        xres_loaded = sem("xres_loaded")
        stored = [sem(f"stored{i}") for i in range(2)]
        split_hi = sem("split_hi")
        split_lo = sem("split_lo")
        consts_ready = sem("consts_ready")
        ident_zero = sem("ident_zero")
        x_squared = sem("x_squared")
        x_mean = sem("x_mean")
        x_rstd_ready = sem("x_rstd_ready")
        xs_ready = sem("xs_ready")
        ht_hi_ready = sem("ht_hi_ready")
        ht_ready = sem("ht_ready")
        unit_done = sem("unit_done")
        unit_read = sem("unit_read")
        unit_freed = sem("unit_freed")
        row_built = sem("row_built")
        row_masked = sem("row_masked")
        lam_dots = sem("lam_dots")
        lam_exps = sem("lam_exps")
        lam_ready = sem("lam_ready")
        score_ready = sem("score_ready")
        logits_ready = sem("logits_ready")
        exp_done = sem("exp_done")
        rsum_ready = sem("rsum_ready")
        ratio_ready = sem("ratio_ready")
        combined = sem("combined")
        pt_ready = sem("pt_ready")
        pt_read = sem("pt_read")
        pt_freed = sem("pt_freed")
        values_done = sem("values_done")
        o_freed = sem("o_freed")
        sub_squared = sem("sub_squared")
        sub_mean = sem("sub_mean")
        sub_rstd_ready = sem("sub_rstd_ready")
        sub_scaled = sem("sub_scaled")
        gate_subln = sem("gate_subln")
        diff_gated = sem("diff_gated")
        gated = sem("gated")
        y_copied = sem("y_copied")
        y_squared = sem("y_squared")
        y_summed = sem("y_summed")
        y_mean = sem("y_mean")
        y_rstd_ready = sem("y_rstd_ready")
        y_scaled = sem("y_scaled")
        y_ready = sem("y_ready")

        block = ctx.enter_context(nc.Block())

        @block.sync
        def _(sp):
            def load_quarter(n):
                if n >= 4:
                    sp.wait_ge(split_lo, n - 3)
                g, k = n // 4, 2 * (n % 4)
                if g < len(GROUPS):
                    col = GROUPS[g][2]
                    src = w_in_v[:, k:k + 2, col:col + WIDTH]
                else:
                    col = (g - len(GROUPS)) * WIDTH
                    src = w_out_v[:, k:k + 2, col:col + WIDTH]
                sp.dma_start(stage[:, n % 4, :].rearrange("p (k n) -> p k n", k=2), src)\
                    .then_inc(w_loaded[n % 4], 16)

            sp.dma_start(x_sb[:, 0, :], x_v[0]).then_inc(x_loaded[0], 16)
            load_quarter(0)
            load_quarter(1)
            for t in range(1, TILES):
                sp.dma_start(x_sb[:, t, :], x_v[t]).then_inc(x_loaded[t], 16)
                if t < 3:
                    load_quarter(t + 1)
            for n in range(4, 8):
                load_quarter(n)
            sp.wait_ge(row_built, 1)
            sp.dma_start(bias_rows.ap(), row_sb).then_inc(rows_stored, 16)
            load_quarter(8)
            sp.wait_ge(rows_stored, 16)
            sp.dma_start(strips[:, :, :], strip_view).then_inc(strips_loaded, 16)
            sp.wait_ge(xs_ready, TILES)
            sp.dma_start(g_row[:, :], norm_post_g[0].partition_broadcast(P)).then_inc(gpost_loaded, 16)
            for n in range(9, QUARTERS):
                load_quarter(n)
            sp.wait_ge(split_lo, QUARTERS)
            sp.dma_start(stage[:, :, :], x[0].rearrange("(t p) d -> p t d", p=P)).then_inc(xres_loaded, 16)
            for i, t in enumerate(DOWN):
                sp.wait_ge(y_ready, i + 1)
                sp.dma_start(out_v[t], y_sb[:, t % 2, :]).then_inc(stored[t % 2], 16)
            for i in range(2):
                sp.wait_ge(stored[i], 16 * (TILES // 2))

        @block.gpsimd
        def _(pool):
            nc.gpsimd.memset(ident[:, :], 0.0).then_inc(ident_zero, 1)
            nc.gpsimd.memset(minus_half[:, :], -0.5).then_inc(consts_ready, 1)
            pool.wait_ge(ident_zero, 1)
            nc.gpsimd.affine_select(out=ident[:, :], in_=ident[:, :], compare_op=ALU.not_equal, fill=1.0,
                                    base=0, pattern=[[-1, P]], channel_multiplier=1).then_inc(consts_ready, 1)
            pool.wait_ge(consts_ready, 2)
            for t in range(TILES):
                pool.wait_ge(x_squared, t + 1)
                nc.gpsimd.tensor_scalar(x_ms[:, t:t + 1], x_sq[:, t:t + 1], 1.0 / DM, NORM_EPS,
                                        ALU.mult, ALU.add).then_inc(x_mean, 1)
                pool.wait_ge(x_mean, t + 1)
                nc.gpsimd.tensor_tensor(x_rstd[:, t:t + 1], x_ms[:, t:t + 1], minus_half[:, 0:1],
                                        ALU.pow).then_inc(x_rstd_ready, 1)
            nc.gpsimd.memset(row_sb[:, 0:P - 1], MASKED).then_inc(row_masked, 1)
            pool.wait_ge(rel_loaded, 16)
            for b in range(BUCKETS):
                lo = first_distance(b)
                hi = first_distance(b + 1) if b + 1 < BUCKETS else SEQ + 1
                last = nc.gpsimd.tensor_copy(row_sb[:, P - 1 + lo:P - 1 + hi],
                                             rel_t[:, b:b + 1].to_broadcast([HEADS, hi - lo]))
                if b == BUCKETS - 1:
                    last.then_inc(row_built, 1)
            pool.wait_ge(small_loaded, 32)
            for t in DOWN:
                pool.wait_ge(unit_freed, UNIT["g", 0, t] + 1)
                g = gates[:, 0, t, :].rearrange("p (h d) -> p h d", h=DIFF_HEADS)
                nc.gpsimd.tensor_tensor(g, g, subln[:, :].unsqueeze(1).to_broadcast([P, DIFF_HEADS, 2 * DH]),
                                        ALU.mult).then_inc(gate_subln, 1)
            keep = (1.0 - LAMBDA_INIT) ** 2
            for i, t in enumerate(DOWN):
                pool.wait_ge(sub_squared, DIFF_HEADS * (i + 1))
                nc.gpsimd.tensor_scalar(sub_ms[:, t, :], sub_sq[:, t, :], 1.0 / (2 * DH * keep),
                                        SUBLN_EPS / keep, ALU.mult, ALU.add).then_inc(sub_mean, 1)
                pool.wait_ge(sub_mean, i + 1)
                nc.gpsimd.tensor_tensor(sub_rstd[:, t, :], sub_ms[:, t, :], minus_half[:, :],
                                        ALU.pow).then_inc(sub_rstd_ready, 1)
            for i, t in enumerate(DOWN):
                pool.wait_ge(y_squared, 2 * (i + 1))
                nc.gpsimd.tensor_tensor(y_sum[:, t:t + 1], y_sq[:, t, 0:1], y_sq[:, t, 1:2],
                                        ALU.add).then_inc(y_summed, 1)
                pool.wait_ge(y_summed, i + 1)
                nc.gpsimd.tensor_scalar(y_ms[:, t:t + 1], y_sum[:, t:t + 1], 1.0 / DM,
                                        NORM_EPS * W_SCALE ** 2, ALU.mult, ALU.add).then_inc(y_mean, 1)
                pool.wait_ge(y_mean, i + 1)
                nc.gpsimd.tensor_tensor(y_rstd[:, t:t + 1], y_ms[:, t:t + 1], minus_half[:, 0:1],
                                        ALU.pow).then_inc(y_rstd_ready, 1)

        @block.tensor
        def _(pe):
            def x_transposes(t):
                pe.wait_ge(xs_ready, t + 1)
                if t >= 2:
                    pe.wait_ge(ht_ready, t - 1)
                for k in range(KT):
                    last = nc.tensor.transpose(xt_banks[t % 2][:, k // 4, (k % 4) * P:(k % 4 + 1) * P],
                                               x_sb[:, t, k * P:(k + 1) * P], ident[:, :])
                last.then_inc(pt_ready if t % 2 == 0 else score_ready, 1)

            def unit_quarter(u, q):
                kind, half, i, g = unit_of(u)
                bank = unit_ps[:, u % 2, :]
                if q == 0:
                    if u >= IN_UNITS + 2:
                        pe.wait_ge(y_copied, u - 1 - IN_UNITS)
                    elif u >= 2:
                        pe.wait_ge(unit_freed, u - 1)
                    if kind == "y":
                        pe.wait_ge(pt_freed, pt_use("a", i) + 1)
                    else:
                        pe.wait_ge(ht_ready, i + 1 if kind in "vg" else TILES)
                pe.wait_ge(split_lo, 4 * g + q + 1)
                for k in (2 * q, 2 * q + 1):
                    wh, wl = w_hi[:, g % 3, k, :], w_lo[:, g % 3, k, :]
                    if kind in "qk":
                        cols = slice(i * P, (i + 1) * P)
                        terms = [(wh[:, cols], ht[:, 0, k, :]), (wh[:, cols], ht[:, 1, k, :]),
                                 (wl[:, cols], ht[:, 0, k, :])]
                    elif kind == "y":
                        ah, al = at[:, i % 2, 0, k, :], at[:, i % 2, 1, k, :]
                        terms = [(ah, wh), (ah, wl), (al, wh)]
                    else:
                        rows = slice(i * P, (i + 1) * P)
                        hh, hl = ht[:, 0, k, rows], ht[:, 1, k, rows]
                        terms = [(hh, wh), (hh, wl), (hl, wh)]
                    for n, (a, b) in enumerate(terms):
                        last = nc.tensor.matmul(bank, a, b, start=(k == 0 and n == 0),
                                                stop=(k == KT - 1 and n == 2))
                if q == 3:
                    last.then_inc(unit_done, 1)

            def scores(i):
                r, t, c = STEPS[i]
                ch, n = r * CHUNKS + c, (t + 1) * P
                pe.wait_ge(unit_freed, max(UNIT["q", r, c], UNIT["k", r, c]) + 1)
                if i >= 1:
                    pe.wait_ge(logits_ready, 2 * i)
                rows = slice(t * P, (t + 1) * P)
                for n_term, (qs, ks) in enumerate(((q_hi, k_hi), (q_hi, k_lo), (q_lo, k_hi))):
                    for m in range(2):
                        part = slice(m * DH, (m + 1) * DH)
                        last = nc.tensor.matmul(score_ps[:, m, 0:n], qs[part, ch, rows], ks[part, ch, 0:n],
                                                start=(n_term == 0), stop=(n_term == 2))
                last.then_inc(score_ready, 1)

            def p_transposes(i):
                r, t, c = STEPS[i]
                if r == 0:
                    pe.wait_ge(combined, i + 1)
                else:
                    pe.wait_ge(exp_done, 2 * (i + 1))
                if pt_use("p", i):
                    pe.wait_ge(pt_freed, pt_use("p", i))
                for m in range(1 + r):
                    for k in range(t + 1):
                        cols = slice(k * P, (k + 1) * P)
                        last = nc.tensor.transpose(pt_ps[:, m, cols], probs[:, i % 2, m, cols], ident[:, :])
                last.then_inc(pt_ready, 1)

            def values(i):
                r, t, c = STEPS[i]
                o = i // 4
                if i % 4 == 0 and o >= 2:
                    pe.wait_ge(o_freed, o - 1)
                pe.wait_ge(unit_freed, UNIT["v", r, t] + 1)
                pe.wait_ge(pt_freed, pt_use("p", i) + 1)
                width = 2 * DH // (1 + r)
                for m in range(1 + r):
                    col = c * P + m * width
                    src = slice(r * WIDTH + col, r * WIDTH + col + width)
                    for k in range(t + 1):
                        ks = slice(k * P, (k + 1) * P)
                        ph, pl = pt_hi[:, i % 2, m, ks], pt_lo[:, i % 2, m, ks]
                        for n, (a, b) in enumerate(((ph, v_hi), (ph, v_lo), (pl, v_hi))):
                            last = nc.tensor.matmul(o_ps[:, o % 2, col:col + width], a, b[:, k, src],
                                                    start=(k == 0 and n == 0), stop=(k == t and n == 2))
                last.then_inc(values_done, 1)

            def a_transposes(t):
                pe.wait_ge(gated, TILES - t)
                pe.wait_ge(pt_freed, pt_use("a", t))
                for e in range(KT):
                    last = nc.tensor.transpose(pt_ps[:, e // 4, (e % 4) * P:(e % 4 + 1) * P],
                                               gates[:, e // 4, t, (e % 4) * P:(e % 4 + 1) * P], ident[:, :])
                last.then_inc(pt_ready, 1)

            pe.wait_ge(consts_ready, 2)
            x_transposes(0)
            x_transposes(1)
            for u in range(3 * TILES):
                for q in range(4):
                    unit_quarter(u, q)
                if u + 2 < TILES:
                    x_transposes(u + 2)
            for j in range(SLOTS):
                if j < NSTEP:
                    scores(j)
                for u, q in FILL[j][0]:
                    unit_quarter(u, q)
                if j >= 2:
                    values(j - 2)
                if 1 <= j <= NSTEP:
                    p_transposes(j - 1)
                for u, q in FILL[j][1]:
                    unit_quarter(u, q)
                for t in DOWN:
                    if AT_SLOT[t] == j:
                        a_transposes(t)
            for u in LAST_UNITS:
                for q in range(4):
                    unit_quarter(u, q)

        @block.scalar
        def _(act):
            last_square = []

            def square(dst, src, done, count):
                if last_square:
                    act.wait_ge(*last_square.pop())
                n = src.shape[-1]
                nc.scalar.activation(junk[:, 0:n], src, ACT.Square, accum_out=dst).then_inc(done, 1)
                last_square.append((done, count))

            def split(n):
                g, k = n // 4, 2 * (n % 4)
                act.wait_ge(w_loaded[n % 4], 16 * (n // 4 + 1))
                if g >= 3:
                    act.wait_ge(unit_done, 4 * (g - 2))
                nc.scalar.activation(w_hi[:, g % 3, k:k + 2, :],
                                     stage[:, n % 4, :].rearrange("p (k n) -> p k n", k=2),
                                     ACT.Copy, scale=W_SCALE).then_inc(split_hi, 1)

            def unit(u):
                kind, r, i, g = unit_of(u)
                if kind == "y":
                    act.wait_ge(y_copied, u - IN_UNITS + 1)
                    square(y_sq[:, i, r:r + 1], y_sb[:, i % 2, r * WIDTH:(r + 1) * WIDTH], y_squared,
                           u - IN_UNITS + 1)
                    return
                act.wait_ge(unit_done, u + 1)
                src = unit_ps[:, u % 2, :]
                if kind == "g":
                    act.wait_ge(unit_freed, u - 1)
                    ins = nc.scalar.activation(tanh_sb[:, u % 2, :], src, ACT.Tanh, scale=0.5 * U_SCALE)
                elif kind == "v":
                    ins = nc.scalar.activation(v_hi[:, i, r * WIDTH:(r + 1) * WIDTH], src, ACT.Copy,
                                               scale=U_SCALE)
                elif kind == "q":
                    ins = nc.scalar.activation(q_hi[:, r * CHUNKS + i, :], src, ACT.Copy, scale=Q_SCALE)
                else:
                    ins = nc.scalar.activation(k_hi[:, r * CHUNKS + i, :], src, ACT.Copy, scale=U_SCALE)
                ins.then_inc(unit_read, 1)

            def x_hi(t):
                if t % 2 == 0:
                    act.wait_ge(pt_ready, t // 2 + 1)
                else:
                    act.wait_ge(score_ready, t // 2 + 1)
                nc.scalar.activation(ht[:, 0, :, t * P:(t + 1) * P],
                                     xt_banks[t % 2][:, :, :].rearrange("p b (k s) -> p (b k) s", s=P),
                                     ACT.Copy).then_inc(ht_hi_ready, 1)

            def exps(i):
                r, t, c = STEPS[i]
                n = (t + 1) * P
                if i >= 2:
                    act.wait_ge(pt_ready, PT_USE["p", i - 2] + 1)
                for m in range(2):
                    act.wait_ge(logits_ready, 2 * i + m + 1)
                    nc.scalar.activation(probs[:, i % 2, m, 0:n], neglog[:, i % 2, m, 0:n], ACT.Exp,
                                         bias=negmax[:, i, m:m + 1], scale=-1.0,
                                         accum_out=sums[:, i, m:m + 1]).then_inc(exp_done, 1)

            def p_hi(i):
                r, t, c = STEPS[i]
                n = (t + 1) * P
                if i >= 2:
                    act.wait_ge(values_done, i - 1)
                act.wait_ge(pt_ready, PT_USE["p", i] + 1)
                nc.scalar.activation(pt_hi[:, i % 2, 0:1 + r, 0:n], pt_ps[:, 0:1 + r, 0:n],
                                     ACT.Copy).then_inc(pt_read, 1)

            def a_hi(t):
                act.wait_ge(pt_ready, PT_USE["a", t] + 1)
                if t < 2:
                    act.wait_ge(unit_done, UNIT["y", 1, t + 2] + 1)
                nc.scalar.activation(at[:, t % 2, 0, :, :].rearrange("p (b k) s -> p b k s", b=2),
                                     pt_ps[:, :, :].rearrange("p b (k s) -> p b k s", s=P),
                                     ACT.Copy, scale=1.0 / GATE_SCALE).then_inc(pt_read, 1)

            act.dma_start(g_row[:, :], norm_pre_g[0].partition_broadcast(P)).then_inc(gpre_loaded, 16)
            with nc.allow_non_contiguous_dma(reason="32 x 12 table, transposed once"):
                act.dma_start(rel_t, rel_bias.rearrange("b h -> h b")).then_inc(rel_loaded, 16)
            act.dma_start(lam_in[:, :, :], diff_lambda[0].partition_broadcast(P)).then_inc(small_loaded, 16)
            act.dma_start(subln[:, :], diff_subln_g[0].partition_broadcast(P)).then_inc(small_loaded, 16)
            for t in range(TILES):
                act.wait_ge(x_loaded[t], 16)
                square(x_sq[:, t:t + 1], x_sb[:, t, :], x_squared, t + 1)
                if t == 0:
                    split(0)
                    split(1)
                if t >= 1:
                    x_hi(t - 1)
                if t in (1, 2):
                    split(t + 1)
            x_hi(TILES - 1)
            act.wait_ge(lam_dots, 2)
            nc.scalar.activation(lam_exp[:, :], lam_dot[:, :], ACT.Exp).then_inc(lam_exps, 1)
            for u in range(3 * TILES):
                split(u + SPLIT_AHEAD)
                unit(u)
            for j in range(SLOTS):
                if j < NSTEP:
                    exps(j)
                if j >= 1 and j <= NSTEP:
                    p_hi(j - 1)
                for n in SPLIT_IN_SLOT[j]:
                    split(n)
                for u in FILL_END[j]:
                    unit(u)
                for (r, t), s in POST_SLOT.items():
                    if s == j and r == 0:
                        act.wait_ge(o_freed, TILES - t)
                        for h in range(DIFF_HEADS):
                            square(sub_sq[:, t, h:h + 1], heads_out[:, h * P:(h + 1) * P], sub_squared,
                                   DIFF_HEADS * (TILES - 1 - t) + h + 1)
                for t in DOWN:
                    if AT_SLOT[t] == j:
                        a_hi(t)
            for u in LAST_UNITS:
                unit(u)

        @block.vector
        def _(dve):
            def split(n):
                g, k = n // 4, 2 * (n % 4)
                dve.wait_ge(split_hi, n + 1)
                nc.vector.scalar_tensor_tensor(w_lo[:, g % 3, k:k + 2, :],
                                               stage[:, n % 4, :].rearrange("p (k n) -> p k n", k=2), W_SCALE,
                                               w_hi[:, g % 3, k:k + 2, :], ALU.mult,
                                               ALU.subtract).then_inc(split_lo, 1)

            def unit(u):
                kind, r, i, g = unit_of(u)
                src = unit_ps[:, u % 2, :]
                if kind == "y":
                    dve.wait_ge(unit_done, u + 1)
                    if i < 2:
                        dve.wait_ge(stored[i % 2], 16)
                    nc.vector.tensor_copy(y_sb[:, i % 2, r * WIDTH:(r + 1) * WIDTH], src)\
                        .then_inc(y_copied, 1)
                    return
                dve.wait_ge(unit_read, u + 1)
                if kind == "g":
                    ins = nc.vector.scalar_tensor_tensor(gates[:, r, i, :], tanh_sb[:, u % 2, :], 1.0, src,
                                                         ALU.add, ALU.mult)
                else:
                    if kind == "v":
                        hi, lo = (a[:, i, r * WIDTH:(r + 1) * WIDTH] for a in (v_hi, v_lo))
                    elif kind == "q":
                        hi, lo = (a[:, r * CHUNKS + i, :] for a in (q_hi, q_lo))
                    else:
                        hi, lo = (a[:, r * CHUNKS + i, :] for a in (k_hi, k_lo))
                    ins = nc.vector.scalar_tensor_tensor(lo, src, Q_SCALE if kind == "q" else U_SCALE, hi,
                                                         ALU.mult, ALU.subtract)
                ins.then_inc(unit_freed, 1)

            def x_norm(t):
                dve.wait_ge(x_rstd_ready, t + 1)
                if t == 0:
                    dve.wait_ge(gpre_loaded, 16)
                nc.vector.scalar_tensor_tensor(x_sb[:, t, :], x_sb[:, t, :], x_rstd[:, t:t + 1], g_row[:, :],
                                               ALU.mult, ALU.mult).then_inc(xs_ready, 1)

            def x_lo(t):
                dve.wait_ge(ht_hi_ready, t + 1)
                last = nc.vector.tensor_tensor(
                    ht[:, 1, :, t * P:(t + 1) * P],
                    xt_banks[t % 2][:, :, :].rearrange("p b (k s) -> p (b k) s", s=P),
                    ht[:, 0, :, t * P:(t + 1) * P], ALU.subtract)
                last.then_inc(ht_ready, 1)

            def logits(i):
                r, t, c = STEPS[i]
                n = (t + 1) * P
                if i >= 2:
                    dve.wait_ge(exp_done, 2 * (i - 1))
                dve.wait_ge(score_ready, X_USES + i + 1)
                for m in range(2):
                    h = c if r == 0 else DIFF_HEADS + 2 * c + m
                    nc.vector.tensor_tensor_reduce(out=neglog[:, i % 2, m, 0:n], in0=score_ps[:, m, 0:n],
                                                   in1=strips[:, h, 0:n][:, ::-1], scale=-1.0, scalar=-MASKED,
                                                   op0=ALU.add, op1=ALU.min,
                                                   accum_out=negmax[:, i, m:m + 1]).then_inc(logits_ready, 1)

            def normalizers(i):
                r, t, c = STEPS[i]
                n = (t + 1) * P
                dve.wait_ge(exp_done, 2 * (i + 1))
                nc.vector.reciprocal(rsums[:, i, :], sums[:, i, :]).then_inc(rsum_ready, 1)
                if r == 0:
                    dve.wait_ge(rsum_ready, i + 1)
                    if i == 0:
                        dve.wait_ge(lam_ready, 1)
                    nc.vector.scalar_tensor_tensor(ratio[:, i:i + 1], rsums[:, i, 1:2], neglam[:, :],
                                                   sums[:, i, 0:1], ALU.mult, ALU.mult).then_inc(ratio_ready, 1)
                    dve.wait_ge(ratio_ready, i + 1)
                    p0, p1 = probs[:, i % 2, 0, 0:n], probs[:, i % 2, 1, 0:n]
                    nc.vector.scalar_tensor_tensor(p0, p1, ratio[:, i:i + 1], p0, ALU.mult,
                                                   ALU.add).then_inc(combined, 1)

            def p_lo(i):
                r, t, c = STEPS[i]
                n = (t + 1) * P
                dve.wait_ge(pt_read, pt_use("p", i) + 1)
                nc.vector.tensor_tensor(pt_lo[:, i % 2, 0:1 + r, 0:n], pt_ps[:, 0:1 + r, 0:n],
                                        pt_hi[:, i % 2, 0:1 + r, 0:n], ALU.subtract).then_inc(pt_freed, 1)

            def a_lo(t):
                dve.wait_ge(pt_read, pt_use("a", t) + 1)
                nc.vector.scalar_tensor_tensor(
                    at[:, t % 2, 1, :, :].rearrange("p k s -> p (k s)"),
                    pt_ps[:, :, :].rearrange("p b n -> p (b n)"), 1.0 / GATE_SCALE,
                    at[:, t % 2, 0, :, :].rearrange("p k s -> p (k s)"), ALU.mult,
                    ALU.subtract).then_inc(pt_freed, 1)

            def head_rows(r, t):
                i0 = r * HALF + 4 * (TILES - 1 - t)
                o = i0 // 4
                dve.wait_ge(values_done, i0 + 4)
                dve.wait_ge(rsum_ready, i0 + 4)
                if o:
                    dve.wait_ge(diff_gated if o <= TILES else gated, o if o <= TILES else o - TILES)
                heads = DIFF_HEADS * (1 + r)
                f = rsums[:, i0:i0 + 4, 0] if r == 0 else rsums[:, i0:i0 + 4, :].rearrange("p i m -> p (i m)")
                nc.vector.tensor_tensor(heads_out[:, :].rearrange("p (h d) -> p h d", h=heads),
                                        o_ps[:, o % 2, :].rearrange("p (h d) -> p h d", h=heads),
                                        f.unsqueeze(2).to_broadcast([P, heads, WIDTH // heads]),
                                        ALU.mult).then_inc(o_freed, 1)
                return o

            def gate_diff(t):
                i = TILES - 1 - t
                dve.wait_ge(sub_rstd_ready, i + 1)
                ho = heads_out[:, :].rearrange("p (h d) -> p h d", h=DIFF_HEADS)
                nc.vector.tensor_tensor(ho, ho,
                                        sub_rstd[:, t, :].unsqueeze(2).to_broadcast([P, DIFF_HEADS, P]),
                                        ALU.mult).then_inc(sub_scaled, 1)
                dve.wait_ge(sub_scaled, i + 1)
                dve.wait_ge(gate_subln, i + 1)
                nc.vector.tensor_tensor(gates[:, 0, t, :], heads_out[:, :], gates[:, 0, t, :],
                                        ALU.mult).then_inc(diff_gated, 1)

            def gate_moba(t):
                o = head_rows(1, t)
                dve.wait_ge(o_freed, o + 1)
                nc.vector.tensor_tensor(gates[:, 1, t, :], heads_out[:, :], gates[:, 1, t, :],
                                        ALU.mult).then_inc(gated, 1)

            def finish_rows(t):
                i = TILES - 1 - t
                dve.wait_ge(y_rstd_ready, i + 1)
                if i == 0:
                    dve.wait_ge(gpost_loaded, 16)
                    dve.wait_ge(xres_loaded, 16)
                row = y_sb[:, t % 2, :]
                nc.vector.scalar_tensor_tensor(row, row, y_rstd[:, t:t + 1], g_row[:, :], ALU.mult,
                                               ALU.mult).then_inc(y_scaled, 1)
                dve.wait_ge(y_scaled, i + 1)
                nc.vector.tensor_tensor(row, row, stage[:, t, :], ALU.add).then_inc(y_ready, 1)

            x_norm(0)
            split(0)
            split(1)
            x_norm(1)
            x_lo(0)
            split(2)
            x_norm(2)
            x_lo(1)
            split(3)
            x_norm(3)
            x_lo(2)
            x_lo(3)
            dve.wait_ge(small_loaded, 32)
            for i in range(2):
                nc.vector.tensor_tensor_reduce(out=lam_junk[:, i, :], in0=lam_in[:, 2 * i, :],
                                               in1=lam_in[:, 2 * i + 1, :], scale=1.0, scalar=0.0,
                                               op0=ALU.mult, op1=ALU.add,
                                               accum_out=lam_dot[:, i:i + 1]).then_inc(lam_dots, 1)
            for u in range(3 * TILES):
                split(u + SPLIT_AHEAD)
                unit(u)
                if u == 2:
                    dve.wait_ge(lam_exps, 1)
                    nc.vector.scalar_tensor_tensor(neglam[:, :], lam_exp[:, 1:2], -LAMBDA_INIT,
                                                   lam_exp[:, 0:1], ALU.add, ALU.subtract)\
                        .then_inc(lam_ready, 1)
            dve.wait_ge(strips_loaded, 16)
            for j in range(SLOTS):
                if j < NSTEP:
                    logits(j)
                if j >= 1 and j <= NSTEP:
                    p_lo(j - 1)
                if j < NSTEP:
                    normalizers(j)
                for (r, t), s in POST_SLOT.items():
                    if s == j and r == 1:
                        gate_moba(t)
                for n in SPLIT_IN_SLOT[j]:
                    split(n)
                for u in FILL_END[j]:
                    unit(u)
                for (r, t), s in POST_SLOT.items():
                    if s == j and r == 0:
                        head_rows(0, t)
                    if s + 1 == j and r == 0:
                        gate_diff(t)
                for t in DOWN:
                    if AT_SLOT[t] == j:
                        a_lo(t)
                for t in DOWN[:-1]:
                    if UNIT["y", 1, t] in (FILL_END[j - 1] if j else []):
                        finish_rows(t)
            for u in LAST_UNITS:
                unit(u)
                if u == LAST_UNITS[0]:
                    finish_rows(1)
            finish_rows(0)


_INS = ["x", "norm_pre_g", "w_in", "diff_lambda", "diff_subln_g", "w_out", "norm_post_g", "rel_bias"]


def kernel(**inputs):
    import numpy as _np
    import concourse.bacc as _bacc
    from concourse import mybir as _mybir
    from concourse.bass_utils import run_bass_kernel_spmd as _run

    nc = _bacc.Bacc("TRN2", target_bir_lowering=False, num_devices=1)
    arrays, args = {}, []
    for name in _INS:
        a = _np.ascontiguousarray(inputs[name])
        arrays[f"in_{name}_dram"] = a
        args.append(nc.dram_tensor(f"in_{name}_dram", a.shape, _mybir.dt.from_np(a.dtype),
                                   kind="ExternalInput").ap())
    shape = arrays["in_x_dram"].shape
    args.append(nc.dram_tensor("out_dram", shape, _mybir.dt.float32, kind="ExternalOutput").ap())
    bass_hymba_diff_moba_layer(nc, *args)
    r = _run(nc, [arrays], core_ids=[0])
    return r.results[0]["out_dram"]
```

```python
import math
from contextlib import ExitStack

import concourse.bass as bass
from concourse import mybir


def bass_hymba_diff_moba_layer(
    nc: bass.Bass,
    x: bass.AP,
    norm_pre_g: bass.AP,
    w_in: bass.AP,
    diff_lambda: bass.AP,
    diff_subln_g: bass.AP,
    w_out: bass.AP,
    norm_post_g: bass.AP,
    rel_bias: bass.AP,
    out: bass.AP,
):
    fp32 = mybir.dt.float32
    fp16 = mybir.dt.float16
    ALU = mybir.AluOpType
    ACT = mybir.ActivationFunctionType

    P = 128
    SEQ, DM = x.shape[1], x.shape[2]
    TILES = SEQ // P
    KT = DM // P
    WIDTH = SEQ
    DH = 64
    CHUNKS = WIDTH // P
    DIFF_HEADS = 4
    HEADS = rel_bias.shape[1]
    BUCKETS = rel_bias.shape[0]
    MAX_DISTANCE = 128
    NORM_EPS, SUBLN_EPS = 1e-6, 1e-5
    LAMBDA_INIT = 0.8 - 0.6 * math.exp(-0.3 * 0)
    MASKED = -3e38

    W_SCALE = 64.0
    Q_SCALE = DH ** -0.5 / W_SCALE
    U_SCALE = 1.0 / W_SCALE
    GATE_SCALE = 2.0 * W_SCALE

    D = WIDTH
    GROUPS = [("v", 0, 2 * D), ("q", 0, 0), ("k", 0, D), ("v", 1, 6 * D), ("k", 1, 5 * D), ("q", 1, 4 * D),
              ("g", 1, 7 * D), ("g", 0, 3 * D)]
    IN_UNITS = len(GROUPS) * TILES
    Y_UNITS = 2 * TILES
    UNITS = IN_UNITS + Y_UNITS
    QUARTERS = 4 * (len(GROUPS) + 2)
    DOWN = list(range(TILES - 1, -1, -1))

    def unit_of(u):
        if u >= IN_UNITS:
            y = u - IN_UNITS
            return "y", y % 2, DOWN[y // 2], len(GROUPS) + y % 2
        kind, region, _ = GROUPS[u // TILES]
        i = u % TILES
        return kind, region, DOWN[i] if kind == "g" else i, u // TILES

    UNIT = {unit_of(u)[:3]: u for u in range(UNITS)}

    STEPS = [(r, t, c) for r in range(2) for t in DOWN for c in range(CHUNKS)]
    NSTEP = len(STEPS)
    SLOTS = NSTEP + 2
    HALF = NSTEP // 2
    FIRST_UNITS = 3 * TILES
    shares = [3] * HALF + [4] * (HALF // 2) + [2] * (HALF // 2) + [4, 2]
    quarters = iter((u, q) for u in range(FIRST_UNITS, UNITS) for q in range(4))
    FILL = [([next(quarters) for _ in range((n + 1) // 2)], [next(quarters) for _ in range(n // 2)])
            for n in shares]
    FILL_END = [[u for part in FILL[j] for u, q in part if q == 3] for j in range(SLOTS)]
    WARM_UP = 10
    FILL_LAST = list(quarters)
    LAST_UNITS = [u for u, q in FILL_LAST if q == 3]
    SPLIT_AHEAD = 4
    SPLIT_IN_SLOT = [[FIRST_UNITS + SPLIT_AHEAD + j] if FIRST_UNITS + SPLIT_AHEAD + j < QUARTERS else []
                     for j in range(SLOTS)]
    AT_SLOT = {(DOWN[i], half): HALF + 4 * (i + 1) + 2 + half for i in range(TILES - 1) for half in range(2)}
    AT_SLOT[0, 0] = AT_SLOT[0, 1] = SLOTS - 1
    AT_ORDER = [(t, half) for t in DOWN for half in range(2)]

    def at_bank(t, half):
        return ((2 * TILES - 1 - t) + (half if t == 0 else 0)) % 2

    POST_SLOT = {STEPS[i][:2]: i + 2 for i in range(NSTEP) if i % 4 == 3}

    PT_ORDER = [("x", 0), ("x", 2)]
    for j in range(SLOTS):
        if 1 <= j <= NSTEP:
            PT_ORDER.append(("p", j - 1))
    PT_USE = {k: n for n, k in enumerate(PT_ORDER)}
    X_USES = 2

    def pt_use(*key):
        return PT_USE[key] - X_USES

    x_v = x[0].rearrange("(t p) d -> t p d", p=P)
    out_v = out[0].rearrange("(t p) d -> t p d", p=P)
    w_in_v = w_in[0].rearrange("(k p) n -> p k n", p=P)
    w_out_v = w_out[0].rearrange("(k p) n -> p k n", p=P)

    ROW = SEQ + P
    bias_rows = nc.dram_tensor("bias_rows", (HEADS, ROW), fp32, kind="Internal")
    strip_view = bass.AP(tensor=bias_rows, offset=0, ap=[[1, P], [ROW, HEADS], [1, SEQ]])

    def first_distance(b):
        exact = BUCKETS // 2
        if b <= exact:
            return b
        return next(n for n in range(exact, SEQ + 1)
                    if n == SEQ or min(exact + int(math.log(n / exact) / math.log(MAX_DISTANCE / exact)
                                                   * (BUCKETS - exact)), BUCKETS - 1) >= b)

    ctx = ExitStack()
    with ctx:
        def sb(name, shape, dt=fp32):
            return ctx.enter_context(nc.sbuf_tensor(name, shape, dt))

        def sem(name):
            return ctx.enter_context(nc.semaphore(name))

        arena = sb("arena", [P, 4 * DM])
        x_sb = arena[:, :].rearrange("p (t d) -> p t d", t=TILES)
        neglog = arena[:, 0:2 * DM].rearrange("p (b m n) -> p b m n", b=2, m=2)
        probs = arena[:, 2 * DM:4 * DM].rearrange("p (b m n) -> p b m n", b=2, m=2)
        area = sb("area", [P, 4 * DM])
        ht = area[:, :].bitcast(fp16).rearrange("p (h k s) -> p h k s", h=2, k=KT)
        y_sb = area[:, 2 * DM:4 * DM].rearrange("p (b d) -> p b d", b=2)
        stage = sb("stage", [P, 4, 2 * WIDTH])
        w_hi = sb("w_hi", [P, 3, KT, WIDTH], fp16)
        w_lo = sb("w_lo", [P, 3, KT, WIDTH], fp16)
        q_hi = sb("q_hi", [P, 2 * CHUNKS, SEQ], fp16)
        q_lo = sb("q_lo", [P, 2 * CHUNKS, SEQ], fp16)
        at_hi = q_hi[:, 0:CHUNKS, :].rearrange("p c (e s) -> p (c e) s", s=P).rearrange("p (b e) s -> p b e s", b=2)
        at_lo = q_lo[:, 0:CHUNKS, :].rearrange("p c (e s) -> p (c e) s", s=P).rearrange("p (b e) s -> p b e s", b=2)
        k_hi = sb("k_hi", [P, 2 * CHUNKS, SEQ], fp16)
        k_lo = sb("k_lo", [P, 2 * CHUNKS, SEQ], fp16)
        v_hi = sb("v_hi", [P, TILES, 2 * WIDTH], fp16)
        v_lo = sb("v_lo", [P, TILES, 2 * WIDTH], fp16)
        gates = sb("gates", [P, 2, TILES, WIDTH])
        strips = sb("strips", [P, HEADS, SEQ])
        pt_hi = sb("pt_hi", [P, 2, 2, SEQ], fp16)
        pt_lo = sb("pt_lo", [P, 2, 2, SEQ], fp16)
        g_row = sb("g_row", [P, DM])
        subln = sb("subln", [P, 2 * DH])
        tanh_sb = sb("tanh_sb", [P, 2, WIDTH])
        heads_out = sb("heads_out", [P, WIDTH])
        junk = sb("junk", [P, DM], fp16)
        ident = sb("ident", [P, P])
        negmax = sb("negmax", [P, NSTEP, 2])
        sums = sb("sums", [P, NSTEP, 2])
        rsums = sb("rsums", [P, NSTEP, 2])
        ratio = sb("ratio", [P, HALF])
        lam_in = sb("lam_in", [P, 4, DH])
        lam_junk = sb("lam_junk", [P, 2, DH])
        lam_dot = sb("lam_dot", [P, 2])
        lam_exp = sb("lam_exp", [P, 2])
        neglam = sb("neglam", [P, 1])
        minus_half = sb("minus_half", [P, 4])
        x_sq = sb("x_sq", [P, TILES])
        x_ms = sb("x_ms", [P, TILES])
        x_rstd = sb("x_rstd", [P, TILES])
        sub_sq = sb("sub_sq", [P, TILES, DIFF_HEADS])
        sub_ms = sb("sub_ms", [P, TILES, DIFF_HEADS])
        sub_rstd = sb("sub_rstd", [P, TILES, DIFF_HEADS])
        y_sq = sb("y_sq", [P, TILES, 2])
        y_part = sb("y_part", [P, TILES])
        y_ms = sb("y_ms", [P, TILES])
        y_rstd = sb("y_rstd", [P, TILES])
        row_sb = tanh_sb[0:HEADS, :, :].rearrange("p b n -> p (b n)")[:, 0:ROW]
        rel_t = tanh_sb[0:HEADS, :, :].rearrange("p b n -> p (b n)")[:, ROW:ROW + BUCKETS]

        unit_ps = ctx.enter_context(nc.psum_tensor("unit_ps", [P, 2, 512], fp32))
        score_ps = ctx.enter_context(nc.psum_tensor("score_ps", [P, 2, 512], fp32))
        pt_ps = ctx.enter_context(nc.psum_tensor("pt_ps", [P, 2, 512], fp32))
        o_ps = ctx.enter_context(nc.psum_tensor("o_ps", [P, 2, 512], fp32))
        xt_banks = [pt_ps, score_ps]

        x_loaded = [sem(f"x_loaded{t}") for t in range(TILES)]
        gpre_loaded = sem("gpre_loaded")
        gpost_loaded = sem("gpost_loaded")
        small_loaded = sem("small_loaded")
        rel_loaded = sem("rel_loaded")
        rows_stored = sem("rows_stored")
        strips_loaded = sem("strips_loaded")
        w_loaded = [sem(f"w_loaded{i}") for i in range(4)]
        xres_loaded = sem("xres_loaded")
        stored = [sem(f"stored{i}") for i in range(2)]
        stored_last = sem("stored_last")
        split_hi = sem("split_hi")
        split_lo = sem("split_lo")
        consts_ready = sem("consts_ready")
        ident_zero = sem("ident_zero")
        x_squared = sem("x_squared")
        x_mean = sem("x_mean")
        x_rstd_ready = sem("x_rstd_ready")
        xs_ready = sem("xs_ready")
        ht_hi_ready = sem("ht_hi_ready")
        ht_ready = sem("ht_ready")
        unit_done = sem("unit_done")
        unit_read = sem("unit_read")
        unit_freed = sem("unit_freed")
        row_built = sem("row_built")
        row_masked = sem("row_masked")
        lam_dots = sem("lam_dots")
        lam_exps = sem("lam_exps")
        lam_ready = sem("lam_ready")
        score_ready = sem("score_ready")
        logits_ready = sem("logits_ready")
        exp_done = sem("exp_done")
        rsum_ready = sem("rsum_ready")
        ratio_ready = sem("ratio_ready")
        combined = sem("combined")
        pt_ready = sem("pt_ready")
        pt_read = sem("pt_read")
        pt_freed = sem("pt_freed")
        values_done = sem("values_done")
        o_freed = sem("o_freed")
        sub_squared = sem("sub_squared")
        sub_mean = sem("sub_mean")
        sub_rstd_ready = sem("sub_rstd_ready")
        sub_scaled = sem("sub_scaled")
        gate_silu = sem("gate_silu")
        diff_gated = sem("diff_gated")
        gated = sem("gated")
        at_turned = sem("at_turned")
        at_read = sem("at_read")
        at_ready = sem("at_ready")
        y_copied = sem("y_copied")
        y_squared = sem("y_squared")
        y_summed = sem("y_summed")
        y_mean = sem("y_mean")
        y_rstd_ready = sem("y_rstd_ready")
        y_scaled = sem("y_scaled")
        y_ready = sem("y_ready")
        y_first_ready = sem("y_first_ready")
        diff_normed = sem("diff_normed")

        block = ctx.enter_context(nc.Block())

        @block.sync
        def _(sp):
            def load_quarter(n):
                if n >= 4:
                    sp.wait_ge(split_lo, n - 3)
                g, k = n // 4, 2 * (n % 4)
                if g < len(GROUPS):
                    col = GROUPS[g][2]
                    src = w_in_v[:, k:k + 2, col:col + WIDTH]
                else:
                    col = (g - len(GROUPS)) * WIDTH
                    src = w_out_v[:, k:k + 2, col:col + WIDTH]
                sp.dma_start(stage[:, n % 4, :].rearrange("p (k n) -> p k n", k=2), src)\
                    .then_inc(w_loaded[n % 4], 16)

            def load_x(t):
                sp.dma_start(x_sb[:, t, :], x_v[t]).then_inc(x_loaded[t], 16)

            load_x(0)
            sp.dma_start(g_row[:, :], norm_pre_g[0].partition_broadcast(P)).then_inc(gpre_loaded, 16)
            load_quarter(0)
            load_quarter(1)
            load_x(1)
            load_quarter(2)
            load_quarter(3)
            load_x(2)
            load_x(3)
            with nc.allow_non_contiguous_dma(reason="32 x 12 table, transposed once"):
                sp.dma_start(rel_t, rel_bias.rearrange("b h -> h b")).then_inc(rel_loaded, 16)
            sp.dma_start(lam_in[:, :, :], diff_lambda[0].partition_broadcast(P)).then_inc(small_loaded, 16)
            sp.dma_start(subln[:, :], diff_subln_g[0].partition_broadcast(P)).then_inc(small_loaded, 16)
            for n in range(4, 8):
                load_quarter(n)
            sp.wait_ge(row_built, 1)
            sp.dma_start(bias_rows.ap(), row_sb).then_inc(rows_stored, 16)
            load_quarter(8)
            sp.wait_ge(rows_stored, 16)
            sp.dma_start(strips[:, :, :], strip_view).then_inc(strips_loaded, 16)
            sp.wait_ge(xs_ready, TILES)
            sp.dma_start(g_row[:, :], norm_post_g[0].partition_broadcast(P)).then_inc(gpost_loaded, 16)
            for n in range(9, QUARTERS):
                load_quarter(n)
            sp.wait_ge(split_lo, QUARTERS)
            sp.dma_start(stage[:, :, :], x[0].rearrange("(t p) d -> p t d", p=P)).then_inc(xres_loaded, 16)
            for i, t in enumerate(DOWN[:-1]):
                sp.wait_ge(y_ready, i + 1)
                sp.dma_start(out_v[t], y_sb[:, t % 2, :]).then_inc(stored[t % 2], 16)
            sp.wait_ge(y_ready, TILES)
            sp.dma_start(out_v[0][:, WIDTH:], y_sb[:, 0, WIDTH:]).then_inc(stored[0], 16)
            sp.wait_ge(y_first_ready, 1)
            sp.dma_start(out_v[0][:, 0:WIDTH], y_sb[:, 0, 0:WIDTH]).then_inc(stored_last, 16)
            sp.wait_ge(stored[0], 16 * 2)
            sp.wait_ge(stored[1], 16 * 2)
            sp.wait_ge(stored_last, 16)

        @block.gpsimd
        def _(pool):
            nc.gpsimd.memset(ident[:, :], 0.0).then_inc(ident_zero, 1)
            nc.gpsimd.memset(minus_half[:, :], -0.5).then_inc(consts_ready, 1)
            pool.wait_ge(ident_zero, 1)
            nc.gpsimd.affine_select(out=ident[:, :], in_=ident[:, :], compare_op=ALU.not_equal, fill=1.0,
                                    base=0, pattern=[[-1, P]], channel_multiplier=1).then_inc(consts_ready, 1)
            pool.wait_ge(consts_ready, 2)
            for t in range(TILES):
                pool.wait_ge(x_squared, t + 1)
                nc.gpsimd.tensor_scalar(x_ms[:, t:t + 1], x_sq[:, t:t + 1], 1.0 / DM, NORM_EPS,
                                        ALU.mult, ALU.add).then_inc(x_mean, 1)
                pool.wait_ge(x_mean, t + 1)
                nc.gpsimd.tensor_tensor(x_rstd[:, t:t + 1], x_ms[:, t:t + 1], minus_half[:, 0:1],
                                        ALU.pow).then_inc(x_rstd_ready, 1)
            nc.gpsimd.memset(row_sb[:, 0:P - 1], MASKED).then_inc(row_masked, 1)
            pool.wait_ge(rel_loaded, 16)
            for b in range(BUCKETS):
                lo = first_distance(b)
                hi = first_distance(b + 1) if b + 1 < BUCKETS else SEQ + 1
                last = nc.gpsimd.tensor_copy(row_sb[:, P - 1 + lo:P - 1 + hi],
                                             rel_t[:, b:b + 1].to_broadcast([HEADS, hi - lo]))
                if b == BUCKETS - 1:
                    last.then_inc(row_built, 1)
            pool.wait_ge(small_loaded, 32)
            keep = (1.0 - LAMBDA_INIT) ** 2
            for i, t in enumerate(DOWN):
                pool.wait_ge(sub_squared, DIFF_HEADS * (i + 1))
                nc.gpsimd.tensor_scalar(sub_ms[:, t, :], sub_sq[:, t, :], 1.0 / (2 * DH * keep),
                                        SUBLN_EPS / keep, ALU.mult, ALU.add).then_inc(sub_mean, 1)
                pool.wait_ge(sub_mean, i + 1)
                nc.gpsimd.tensor_tensor(sub_rstd[:, t, :], sub_ms[:, t, :], minus_half[:, :],
                                        ALU.pow).then_inc(sub_rstd_ready, 1)
                pool.wait_ge(sub_rstd_ready, i + 1)
                rows = gates[:, 0, t, :].rearrange("p (h d) -> p h d", h=DIFF_HEADS)
                nc.gpsimd.tensor_tensor(rows, rows, sub_rstd[:, t, :].unsqueeze(2).to_broadcast([P, DIFF_HEADS, P]),
                                        ALU.mult).then_inc(sub_scaled, 1)
                pool.wait_ge(sub_scaled, i + 1)
                nc.gpsimd.tensor_tensor(rows, rows, subln[:, :].unsqueeze(1).to_broadcast([P, DIFF_HEADS, P]),
                                        ALU.mult).then_inc(diff_normed, 1)
            for i, t in enumerate(DOWN):
                pool.wait_ge(y_squared, 2 * i + 1)
                nc.gpsimd.tensor_scalar(y_part[:, t:t + 1], y_sq[:, t, 0:1], 1.0 / DM,
                                        NORM_EPS * W_SCALE ** 2, ALU.mult, ALU.add).then_inc(y_summed, 1)
                pool.wait_ge(y_summed, i + 1)
                pool.wait_ge(y_squared, 2 * (i + 1))
                nc.gpsimd.tensor_scalar(y_ms[:, t:t + 1], y_sq[:, t, 1:2], 1.0 / DM, y_part[:, t:t + 1],
                                        ALU.mult, ALU.add).then_inc(y_mean, 1)
                pool.wait_ge(y_mean, i + 1)
                nc.gpsimd.tensor_tensor(y_rstd[:, t:t + 1], y_ms[:, t:t + 1], minus_half[:, 0:1],
                                        ALU.pow).then_inc(y_rstd_ready, 1)
            pool.wait_ge(y_scaled, TILES)
            nc.gpsimd.tensor_tensor(y_sb[:, 0, 0:WIDTH], y_sb[:, 0, 0:WIDTH], stage[:, 0, 0:WIDTH],
                                    ALU.add).then_inc(y_first_ready, 1)

        @block.tensor
        def _(pe):
            def x_transposes(t):
                pe.wait_ge(xs_ready, t + 1)
                if t >= 2:
                    pe.wait_ge(ht_ready, t - 1)
                for k in range(KT):
                    last = nc.tensor.transpose(xt_banks[t % 2][:, k // 4, (k % 4) * P:(k % 4 + 1) * P],
                                               x_sb[:, t, k * P:(k + 1) * P], ident[:, :])
                last.then_inc(pt_ready if t % 2 == 0 else score_ready, 1)

            def unit_quarter(u, q):
                kind, half, i, g = unit_of(u)
                bank = unit_ps[:, u % 2, :]
                if q == 0:
                    if u >= IN_UNITS + 2:
                        pe.wait_ge(y_copied, u - 1 - IN_UNITS)
                    elif u >= 2:
                        pe.wait_ge(unit_freed, u - 1)
                    if kind == "y":
                        pe.wait_ge(at_ready, 2 * (TILES - i))
                    else:
                        pe.wait_ge(ht_ready, i + 1 if kind in "vg" else TILES)
                pe.wait_ge(split_lo, 4 * g + q + 1)
                for k in (2 * q, 2 * q + 1):
                    wh, wl = w_hi[:, g % 3, k, :], w_lo[:, g % 3, k, :]
                    if kind in "qk":
                        cols = slice(i * P, (i + 1) * P)
                        terms = [(wh[:, cols], ht[:, 0, k, :]), (wh[:, cols], ht[:, 1, k, :]),
                                 (wl[:, cols], ht[:, 0, k, :])]
                    elif kind == "y":
                        ah, al = at_hi[:, i % 2, k, :], at_lo[:, i % 2, k, :]
                        terms = [(ah, wh), (ah, wl), (al, wh)]
                    else:
                        rows = slice(i * P, (i + 1) * P)
                        hh, hl = ht[:, 0, k, rows], ht[:, 1, k, rows]
                        terms = [(hh, wh), (hh, wl), (hl, wh)]
                    for n, (a, b) in enumerate(terms):
                        last = nc.tensor.matmul(bank, a, b, start=(k == 0 and n == 0),
                                                stop=(k == KT - 1 and n == 2))
                if q == 3:
                    last.then_inc(unit_done, 1)

            def scores(i):
                r, t, c = STEPS[i]
                ch, n = r * CHUNKS + c, (t + 1) * P
                pe.wait_ge(unit_freed, max(UNIT["q", r, c], UNIT["k", r, c]) + 1)
                if i >= 1:
                    pe.wait_ge(logits_ready, 2 * i)
                rows = slice(t * P, (t + 1) * P)
                for n_term, (qs, ks) in enumerate(((q_hi, k_hi), (q_hi, k_lo), (q_lo, k_hi))):
                    for m in range(2):
                        part = slice(m * DH, (m + 1) * DH)
                        last = nc.tensor.matmul(score_ps[:, m, 0:n], qs[part, ch, rows], ks[part, ch, 0:n],
                                                start=(n_term == 0), stop=(n_term == 2))
                last.then_inc(score_ready, 1)

            def p_transposes(i):
                r, t, c = STEPS[i]
                if r == 0:
                    pe.wait_ge(combined, i + 1)
                else:
                    pe.wait_ge(exp_done, 2 * (i + 1))
                if pt_use("p", i):
                    pe.wait_ge(pt_freed, pt_use("p", i))
                for m in range(1 + r):
                    for k in range(t + 1):
                        cols = slice(k * P, (k + 1) * P)
                        last = nc.tensor.transpose(pt_ps[:, m, cols], probs[:, i % 2, m, cols], ident[:, :])
                last.then_inc(pt_ready, 1)

            def values(i):
                r, t, c = STEPS[i]
                o = i // 4
                if i % 4 == 0 and o >= 2:
                    pe.wait_ge(o_freed, o - 1)
                pe.wait_ge(unit_freed, UNIT["v", r, t] + 1)
                pe.wait_ge(pt_freed, pt_use("p", i) + 1)
                width = 2 * DH // (1 + r)
                for m in range(1 + r):
                    col = c * P + m * width
                    src = slice(r * WIDTH + col, r * WIDTH + col + width)
                    for k in range(t + 1):
                        ks = slice(k * P, (k + 1) * P)
                        ph, pl = pt_hi[:, i % 2, m, ks], pt_lo[:, i % 2, m, ks]
                        for n, (a, b) in enumerate(((ph, v_hi), (ph, v_lo), (pl, v_hi))):
                            last = nc.tensor.matmul(o_ps[:, o % 2, col:col + width], a, b[:, k, src],
                                                    start=(k == 0 and n == 0), stop=(k == t and n == 2))
                last.then_inc(values_done, 1)

            def a_transposes(t, half):
                pe.wait_ge(gated, TILES - t)
                pe.wait_ge(diff_gated, TILES - t)
                n = AT_ORDER.index((t, half))
                if half and t:
                    pe.wait_ge(at_ready, n)
                for e in range(CHUNKS):
                    cols = slice(e * P, (e + 1) * P)
                    last = nc.tensor.transpose(o_ps[:, at_bank(t, half), cols], gates[:, half, t, cols],
                                               ident[:, :])
                last.then_inc(at_turned, 1)

            pe.wait_ge(consts_ready, 2)
            for _ in range(WARM_UP):
                nc.tensor.matmul(unit_ps[:, 1, 0:P], ident[:, :], ident[:, :], start=True, stop=True)
            x_transposes(0)
            for u in range(FIRST_UNITS):
                for q in range(4):
                    unit_quarter(u, q)
                    if (u, q) == (0, 1):
                        x_transposes(1)
                if u + 2 < TILES:
                    x_transposes(u + 2)
            for j in range(SLOTS):
                if j < NSTEP:
                    scores(j)
                for u, q in FILL[j][0]:
                    unit_quarter(u, q)
                if j >= 2:
                    values(j - 2)
                if 1 <= j <= NSTEP:
                    p_transposes(j - 1)
                for u, q in FILL[j][1]:
                    unit_quarter(u, q)
                for t, half in AT_ORDER:
                    if AT_SLOT[t, half] == j:
                        a_transposes(t, half)
            for u, q in FILL_LAST:
                unit_quarter(u, q)

        @block.scalar
        def _(act):
            last_square = []

            def square(dst, src, done, count):
                if last_square:
                    act.wait_ge(*last_square.pop())
                n = src.shape[-1]
                nc.scalar.activation(junk[:, 0:n], src, ACT.Square, accum_out=dst).then_inc(done, 1)
                last_square.append((done, count))

            def split(n):
                g, k = n // 4, 2 * (n % 4)
                act.wait_ge(w_loaded[n % 4], 16 * (n // 4 + 1))
                if g >= 3:
                    act.wait_ge(unit_done, 4 * (g - 2))
                nc.scalar.activation(w_hi[:, g % 3, k:k + 2, :],
                                     stage[:, n % 4, :].rearrange("p (k n) -> p k n", k=2),
                                     ACT.Copy, scale=W_SCALE).then_inc(split_hi, 1)

            def unit(u):
                kind, r, i, g = unit_of(u)
                if kind == "y" and i == 0:
                    act.wait_ge(unit_done, u + 1)
                    square(y_sq[:, i, r:r + 1], unit_ps[:, u % 2, :], y_squared, u - IN_UNITS + 1)
                    return
                if kind == "y":
                    act.wait_ge(y_copied, u - IN_UNITS + 1)
                    square(y_sq[:, i, r:r + 1], y_sb[:, i % 2, r * WIDTH:(r + 1) * WIDTH], y_squared,
                           u - IN_UNITS + 1)
                    return
                act.wait_ge(unit_done, u + 1)
                src = unit_ps[:, u % 2, :]
                if kind == "g":
                    act.wait_ge(unit_freed, u - 1)
                    if r == 0 and TILES - 1 - i >= 2:
                        act.wait_ge(diff_gated, TILES - 2 - i)
                    ins = nc.scalar.activation(tanh_sb[:, u % 2, :], src, ACT.Tanh, scale=0.5 * U_SCALE)
                elif kind == "v":
                    ins = nc.scalar.activation(v_hi[:, i, r * WIDTH:(r + 1) * WIDTH], src, ACT.Copy,
                                               scale=U_SCALE)
                elif kind == "q":
                    ins = nc.scalar.activation(q_hi[:, r * CHUNKS + i, :], src, ACT.Copy, scale=Q_SCALE)
                else:
                    ins = nc.scalar.activation(k_hi[:, r * CHUNKS + i, :], src, ACT.Copy, scale=U_SCALE)
                ins.then_inc(unit_read, 1)

            def x_hi(t):
                if t % 2 == 0:
                    act.wait_ge(pt_ready, t // 2 + 1)
                else:
                    act.wait_ge(score_ready, t // 2 + 1)
                nc.scalar.activation(ht[:, 0, :, t * P:(t + 1) * P],
                                     xt_banks[t % 2][:, :, :].rearrange("p b (k s) -> p (b k) s", s=P),
                                     ACT.Copy).then_inc(ht_hi_ready, 1)

            def exps(i):
                r, t, c = STEPS[i]
                n = (t + 1) * P
                if i >= 2:
                    act.wait_ge(pt_ready, PT_USE["p", i - 2] + 1)
                for m in range(2):
                    act.wait_ge(logits_ready, 2 * i + m + 1)
                    nc.scalar.activation(probs[:, i % 2, m, 0:n], neglog[:, i % 2, m, 0:n], ACT.Exp,
                                         bias=negmax[:, i, m:m + 1], scale=-1.0,
                                         accum_out=sums[:, i, m:m + 1]).then_inc(exp_done, 1)

            def p_hi(i):
                r, t, c = STEPS[i]
                n = (t + 1) * P
                if i >= 2:
                    act.wait_ge(values_done, i - 1)
                act.wait_ge(pt_ready, PT_USE["p", i] + 1)
                nc.scalar.activation(pt_hi[:, i % 2, 0:1 + r, 0:n], pt_ps[:, 0:1 + r, 0:n],
                                     ACT.Copy).then_inc(pt_read, 1)

            def a_hi(t, half):
                n = AT_ORDER.index((t, half))
                act.wait_ge(at_turned, n + 1)
                if t < 2:
                    act.wait_ge(unit_done, UNIT["y", 1, t + 2] + 1)
                nc.scalar.activation(at_hi[:, t % 2, half * CHUNKS:(half + 1) * CHUNKS, :],
                                     o_ps[:, at_bank(t, half), :].rearrange("p (e s) -> p e s", s=P),
                                     ACT.Copy, scale=1.0 / GATE_SCALE).then_inc(at_read, 1)

            def x_square(t):
                act.wait_ge(x_loaded[t], 16)
                square(x_sq[:, t:t + 1], x_sb[:, t, :], x_squared, t + 1)

            x_square(0)
            split(0)
            x_hi(0)
            split(1)
            x_square(1)
            split(2)
            split(3)
            x_hi(1)
            x_square(2)
            x_square(3)
            for u in range(FIRST_UNITS):
                if u + 2 < TILES:
                    x_hi(u + 2)
                split(u + SPLIT_AHEAD)
                unit(u)
                if u == 2:
                    act.wait_ge(lam_dots, 2)
                    nc.scalar.activation(lam_exp[:, :], lam_dot[:, :], ACT.Exp).then_inc(lam_exps, 1)
            for j in range(SLOTS):
                if j < NSTEP:
                    exps(j)
                if j >= 1 and j <= NSTEP:
                    p_hi(j - 1)
                for n in SPLIT_IN_SLOT[j]:
                    split(n)
                for u in FILL_END[j]:
                    unit(u)
                for (r, t), s in POST_SLOT.items():
                    if s == j and r == 0:
                        act.wait_ge(o_freed, TILES - t)
                        for h in range(DIFF_HEADS):
                            square(sub_sq[:, t, h:h + 1], gates[:, 0, t, h * P:(h + 1) * P], sub_squared,
                                   DIFF_HEADS * (TILES - 1 - t) + h + 1)
                for t, half in AT_ORDER:
                    if AT_SLOT[t, half] == j:
                        a_hi(t, half)
            for u in LAST_UNITS:
                unit(u)

        @block.vector
        def _(dve):
            def split(n):
                g, k = n // 4, 2 * (n % 4)
                dve.wait_ge(split_hi, n + 1)
                nc.vector.scalar_tensor_tensor(w_lo[:, g % 3, k:k + 2, :],
                                               stage[:, n % 4, :].rearrange("p (k n) -> p k n", k=2), W_SCALE,
                                               w_hi[:, g % 3, k:k + 2, :], ALU.mult,
                                               ALU.subtract).then_inc(split_lo, 1)

            def unit(u):
                kind, r, i, g = unit_of(u)
                src = unit_ps[:, u % 2, :]
                if kind == "y":
                    dve.wait_ge(unit_done, u + 1)
                    if i < 2:
                        dve.wait_ge(stored[i % 2], 16)
                    nc.vector.tensor_copy(y_sb[:, i % 2, r * WIDTH:(r + 1) * WIDTH], src)\
                        .then_inc(y_copied, 1)
                    return
                dve.wait_ge(unit_read, u + 1)
                if kind == "g" and r == 0:
                    nc.vector.scalar_tensor_tensor(tanh_sb[:, u % 2, :], tanh_sb[:, u % 2, :], 1.0, src,
                                                   ALU.add, ALU.mult).then_inc(unit_freed, 1)
                    dve.wait_ge(unit_freed, u + 1)
                    dve.wait_ge(diff_normed, TILES - i)
                    nc.vector.tensor_tensor(gates[:, 0, i, :], gates[:, 0, i, :], tanh_sb[:, u % 2, :],
                                            ALU.mult).then_inc(diff_gated, 1)
                    return
                if kind == "g":
                    ins = nc.vector.scalar_tensor_tensor(gates[:, r, i, :], tanh_sb[:, u % 2, :], 1.0, src,
                                                         ALU.add, ALU.mult)
                else:
                    if kind == "v":
                        hi, lo = (a[:, i, r * WIDTH:(r + 1) * WIDTH] for a in (v_hi, v_lo))
                    elif kind == "q":
                        hi, lo = (a[:, r * CHUNKS + i, :] for a in (q_hi, q_lo))
                    else:
                        hi, lo = (a[:, r * CHUNKS + i, :] for a in (k_hi, k_lo))
                    ins = nc.vector.scalar_tensor_tensor(lo, src, Q_SCALE if kind == "q" else U_SCALE, hi,
                                                         ALU.mult, ALU.subtract)
                ins.then_inc(unit_freed, 1)

            def x_norm(t):
                dve.wait_ge(x_rstd_ready, t + 1)
                if t == 0:
                    dve.wait_ge(gpre_loaded, 16)
                nc.vector.scalar_tensor_tensor(x_sb[:, t, :], x_sb[:, t, :], x_rstd[:, t:t + 1], g_row[:, :],
                                               ALU.mult, ALU.mult).then_inc(xs_ready, 1)

            def x_lo(t):
                dve.wait_ge(ht_hi_ready, t + 1)
                last = nc.vector.tensor_tensor(
                    ht[:, 1, :, t * P:(t + 1) * P],
                    xt_banks[t % 2][:, :, :].rearrange("p b (k s) -> p (b k) s", s=P),
                    ht[:, 0, :, t * P:(t + 1) * P], ALU.subtract)
                last.then_inc(ht_ready, 1)

            def logits(i):
                r, t, c = STEPS[i]
                n = (t + 1) * P
                if i >= 2:
                    dve.wait_ge(exp_done, 2 * (i - 1))
                dve.wait_ge(score_ready, X_USES + i + 1)
                for m in range(2):
                    h = c if r == 0 else DIFF_HEADS + 2 * c + m
                    nc.vector.tensor_tensor_reduce(out=neglog[:, i % 2, m, 0:n], in0=score_ps[:, m, 0:n],
                                                   in1=strips[:, h, 0:n][:, ::-1], scale=-1.0, scalar=-MASKED,
                                                   op0=ALU.add, op1=ALU.min,
                                                   accum_out=negmax[:, i, m:m + 1]).then_inc(logits_ready, 1)

            def normalizers(i):
                r, t, c = STEPS[i]
                n = (t + 1) * P
                dve.wait_ge(exp_done, 2 * (i + 1))
                nc.vector.reciprocal(rsums[:, i, :], sums[:, i, :]).then_inc(rsum_ready, 1)
                if r == 0:
                    dve.wait_ge(rsum_ready, i + 1)
                    if i == 0:
                        dve.wait_ge(lam_ready, 1)
                    nc.vector.scalar_tensor_tensor(ratio[:, i:i + 1], rsums[:, i, 1:2], neglam[:, :],
                                                   sums[:, i, 0:1], ALU.mult, ALU.mult).then_inc(ratio_ready, 1)
                    dve.wait_ge(ratio_ready, i + 1)
                    p0, p1 = probs[:, i % 2, 0, 0:n], probs[:, i % 2, 1, 0:n]
                    nc.vector.scalar_tensor_tensor(p0, p1, ratio[:, i:i + 1], p0, ALU.mult,
                                                   ALU.add).then_inc(combined, 1)

            def p_lo(i):
                r, t, c = STEPS[i]
                n = (t + 1) * P
                dve.wait_ge(pt_read, pt_use("p", i) + 1)
                nc.vector.tensor_tensor(pt_lo[:, i % 2, 0:1 + r, 0:n], pt_ps[:, 0:1 + r, 0:n],
                                        pt_hi[:, i % 2, 0:1 + r, 0:n], ALU.subtract).then_inc(pt_freed, 1)

            def a_lo(t, half):
                dve.wait_ge(at_read, AT_ORDER.index((t, half)) + 1)
                chunks = slice(half * CHUNKS, (half + 1) * CHUNKS)
                nc.vector.scalar_tensor_tensor(
                    at_lo[:, t % 2, chunks, :].rearrange("p e s -> p (e s)"), o_ps[:, at_bank(t, half), :],
                    1.0 / GATE_SCALE, at_hi[:, t % 2, chunks, :].rearrange("p e s -> p (e s)"), ALU.mult,
                    ALU.subtract).then_inc(at_ready, 1)

            def head_rows(r, t, dst):
                i0 = r * HALF + 4 * (TILES - 1 - t)
                o = i0 // 4
                dve.wait_ge(values_done, i0 + 4)
                dve.wait_ge(rsum_ready, i0 + 4)
                heads = DIFF_HEADS * (1 + r)
                f = rsums[:, i0:i0 + 4, 0] if r == 0 else rsums[:, i0:i0 + 4, :].rearrange("p i m -> p (i m)")
                nc.vector.tensor_tensor(dst.rearrange("p (h d) -> p h d", h=heads),
                                        o_ps[:, o % 2, :].rearrange("p (h d) -> p h d", h=heads),
                                        f.unsqueeze(2).to_broadcast([P, heads, WIDTH // heads]),
                                        ALU.mult).then_inc(o_freed, 1)

            def gate_moba(t):
                i = TILES - 1 - t
                if i:
                    dve.wait_ge(gated, i)
                head_rows(1, t, heads_out[:, :])
                dve.wait_ge(o_freed, TILES + i + 1)
                nc.vector.tensor_tensor(gates[:, 1, t, :], heads_out[:, :], gates[:, 1, t, :],
                                        ALU.mult).then_inc(gated, 1)

            def finish_rows(t):
                i = TILES - 1 - t
                dve.wait_ge(y_rstd_ready, i + 1)
                if i == 0:
                    dve.wait_ge(gpost_loaded, 16)
                    dve.wait_ge(xres_loaded, 16)
                row = y_sb[:, t % 2, :]
                nc.vector.scalar_tensor_tensor(row, row, y_rstd[:, t:t + 1], g_row[:, :], ALU.mult,
                                               ALU.mult).then_inc(y_scaled, 1)
                dve.wait_ge(y_scaled, i + 1)
                nc.vector.tensor_tensor(row, row, stage[:, t, :], ALU.add).then_inc(y_ready, 1)

            def finish_last_rows():
                dve.wait_ge(y_rstd_ready, TILES)
                dve.wait_ge(unit_done, UNITS)
                dve.wait_ge(stored[0], 16)
                for half in range(2):
                    cols = slice(half * WIDTH, (half + 1) * WIDTH)
                    nc.vector.scalar_tensor_tensor(y_sb[:, 0, cols], unit_ps[:, half, :], y_rstd[:, 0:1],
                                                   g_row[:, cols], ALU.mult, ALU.mult).then_inc(y_scaled, 1)
                dve.wait_ge(y_scaled, TILES + 1)
                nc.vector.tensor_tensor(y_sb[:, 0, WIDTH:], y_sb[:, 0, WIDTH:], stage[:, 0, WIDTH:],
                                        ALU.add).then_inc(y_ready, 1)

            x_norm(0)
            split(0)
            x_lo(0)
            split(1)
            x_norm(1)
            split(2)
            split(3)
            x_lo(1)
            x_norm(2)
            x_norm(3)
            dve.wait_ge(small_loaded, 32)
            for i in range(2):
                nc.vector.tensor_tensor_reduce(out=lam_junk[:, i, :], in0=lam_in[:, 2 * i, :],
                                               in1=lam_in[:, 2 * i + 1, :], scale=1.0, scalar=0.0,
                                               op0=ALU.mult, op1=ALU.add,
                                               accum_out=lam_dot[:, i:i + 1]).then_inc(lam_dots, 1)
            for u in range(FIRST_UNITS):
                if u + 2 < TILES:
                    x_lo(u + 2)
                split(u + SPLIT_AHEAD)
                unit(u)
                if u == 2:
                    dve.wait_ge(lam_exps, 1)
                    nc.vector.scalar_tensor_tensor(neglam[:, :], lam_exp[:, 1:2], -LAMBDA_INIT,
                                                   lam_exp[:, 0:1], ALU.add, ALU.subtract)\
                        .then_inc(lam_ready, 1)
            dve.wait_ge(strips_loaded, 16)
            for j in range(SLOTS):
                if j < NSTEP:
                    logits(j)
                if j >= 1 and j <= NSTEP:
                    p_lo(j - 1)
                if j < NSTEP:
                    normalizers(j)
                for (r, t), s in POST_SLOT.items():
                    if s == j and r == 1:
                        gate_moba(t)
                for n in SPLIT_IN_SLOT[j]:
                    split(n)
                for u in FILL_END[j]:
                    unit(u)
                for (r, t), s in POST_SLOT.items():
                    if s == j and r == 0:
                        head_rows(0, t, gates[:, 0, t, :])
                for t, half in AT_ORDER:
                    if AT_SLOT[t, half] == j:
                        a_lo(t, half)
                for t in DOWN[:-1]:
                    if UNIT["y", 1, t] in (FILL_END[j - 1] if j else []):
                        finish_rows(t)
            unit(LAST_UNITS[0])
            finish_rows(1)
            finish_last_rows()


_INS = ["x", "norm_pre_g", "w_in", "diff_lambda", "diff_subln_g", "w_out", "norm_post_g", "rel_bias"]


def kernel(**inputs):
    import numpy as _np
    import concourse.bacc as _bacc
    from concourse import mybir as _mybir
    from concourse.bass_utils import run_bass_kernel_spmd as _run

    nc = _bacc.Bacc("TRN2", target_bir_lowering=False, num_devices=1)
    arrays, args = {}, []
    for name in _INS:
        a = _np.ascontiguousarray(inputs[name])
        arrays[f"in_{name}_dram"] = a
        args.append(nc.dram_tensor(f"in_{name}_dram", a.shape, _mybir.dt.from_np(a.dtype),
                                   kind="ExternalInput").ap())
    shape = arrays["in_x_dram"].shape
    args.append(nc.dram_tensor("out_dram", shape, _mybir.dt.float32, kind="ExternalOutput").ap())
    bass_hymba_diff_moba_layer(nc, *args)
    r = _run(nc, [arrays], core_ids=[0])
    return r.results[0]["out_dram"]
```

```python
import math
from contextlib import ExitStack

import concourse.bass as bass
from concourse import mybir


def bass_hymba_diff_moba_layer(
    nc: bass.Bass,
    x: bass.AP,
    norm_pre_g: bass.AP,
    w_in: bass.AP,
    diff_lambda: bass.AP,
    diff_subln_g: bass.AP,
    w_out: bass.AP,
    norm_post_g: bass.AP,
    rel_bias: bass.AP,
    out: bass.AP,
):
    fp32 = mybir.dt.float32
    fp16 = mybir.dt.float16
    ALU = mybir.AluOpType
    ACT = mybir.ActivationFunctionType

    P = 128
    SEQ, DM = x.shape[1], x.shape[2]
    TILES = SEQ // P
    KT = DM // P
    WIDTH = SEQ
    DH = 64
    CHUNKS = WIDTH // P
    DIFF_HEADS = 4
    HEADS = rel_bias.shape[1]
    BUCKETS = rel_bias.shape[0]
    MAX_DISTANCE = 128
    NORM_EPS, SUBLN_EPS = 1e-6, 1e-5
    LAMBDA_INIT = 0.8 - 0.6 * math.exp(-0.3 * 0)
    MASKED = -3e38

    W_SCALE = 64.0
    Q_SCALE = DH ** -0.5 / W_SCALE
    U_SCALE = 1.0 / W_SCALE
    ROOT_MEAN = DM ** -0.5
    GATE_SCALE = 2.0 * W_SCALE

    D = WIDTH
    GROUPS = [("v", 0, 2 * D), ("q", 0, 0), ("k", 0, D), ("v", 1, 6 * D), ("q", 1, 4 * D), ("k", 1, 5 * D),
              ("g", 1, 7 * D), ("g", 0, 3 * D)]
    IN_UNITS = len(GROUPS) * TILES
    Y_UNITS = 2 * TILES
    UNITS = IN_UNITS + Y_UNITS
    QUARTERS = 4 * (len(GROUPS) + 2)
    DOWN = list(range(TILES - 1, -1, -1))

    def unit_of(u):
        if u >= IN_UNITS:
            y = u - IN_UNITS
            return "y", y % 2, DOWN[y // 2], len(GROUPS) + y % 2
        kind, region, _ = GROUPS[u // TILES]
        i = u % TILES
        return kind, region, DOWN[i] if kind == "g" else i, u // TILES

    UNIT = {unit_of(u)[:3]: u for u in range(UNITS)}

    STEPS = [(r, t, c) for r in range(2) for t in DOWN for c in range(CHUNKS)]
    NSTEP = len(STEPS)
    SLOTS = NSTEP + 2
    HALF = NSTEP // 2
    FIRST_UNITS = 3 * TILES
    shares = [(2, 1)] * HALF + [(2, 2)] * (HALF // 2) + [(1, 1)] * (HALF // 2) + [(2, 2), (0, 2)]
    quarters = iter((u, q) for u in range(FIRST_UNITS, UNITS) for q in range(4))
    FILL = [tuple([next(quarters) for _ in range(n)] for n in share) for share in shares]
    FILL_END = [[u for part in FILL[j] for u, q in part if q == 3] for j in range(SLOTS)]
    WARM_UP = (10, 8)
    XRES_SLOT = NSTEP - 7
    FILL_LAST = list(quarters)
    LAST_UNITS = [u for u, q in FILL_LAST if q == 3]
    SPLIT_AHEAD = 4
    SPLIT_IN_SLOT = [[FIRST_UNITS + SPLIT_AHEAD + j] if FIRST_UNITS + SPLIT_AHEAD + j < QUARTERS else []
                     for j in range(SLOTS)]
    AT_HALF = {HALF + 4 * (i + 1) + 2 + half: (DOWN[i], half) for i in range(TILES - 1) for half in range(2)}
    AT_ORDER = [(t, half) for t in DOWN for half in range(2)]

    def at_bank(t, half):
        return ((2 * TILES - 1 - t) + (half if t == 0 else 0)) % 2

    TWICE_SLOT = {4 * m - 3: m for m in range(1, 2 * TILES)}
    K_UNITS = [u for u in range(IN_UNITS) if unit_of(u)[0] == "k"]

    POST_SLOT = {STEPS[i][:2]: i + 2 for i in range(NSTEP) if i % 4 == 3}

    PT_ORDER_X = [("x", 0, 0), ("x", 0, 1), ("x", 2, 0)]
    SCORE_USES_X = 2
    PT_ORDER = list(PT_ORDER_X)
    for j in range(SLOTS):
        if 1 <= j <= NSTEP:
            PT_ORDER.append(("p", j - 1))
    PT_USE = {k: n for n, k in enumerate(PT_ORDER)}
    X_USES = len(PT_ORDER_X)
    X_PARTS = [2] + [1] * (TILES - 1)

    def x_count(t, part=0):
        return sum(X_PARTS[:t]) + part + 1

    def pt_use(*key):
        return PT_USE[key] - X_USES

    x_v = x[0].rearrange("(t p) d -> t p d", p=P)
    out_v = out[0].rearrange("(t p) d -> t p d", p=P)
    w_in_v = w_in[0].rearrange("(k p) n -> p k n", p=P)
    w_out_v = w_out[0].rearrange("(k p) n -> p k n", p=P)

    ROW = SEQ + P
    bias_rows = nc.dram_tensor("bias_rows", (HEADS, ROW), fp32, kind="Internal")
    strip_view = bass.AP(tensor=bias_rows, offset=0, ap=[[1, P], [ROW, HEADS], [1, SEQ]])

    def first_distance(b):
        exact = BUCKETS // 2
        if b <= exact:
            return b
        return next(n for n in range(exact, SEQ + 1)
                    if n == SEQ or min(exact + int(math.log(n / exact) / math.log(MAX_DISTANCE / exact)
                                                   * (BUCKETS - exact)), BUCKETS - 1) >= b)

    ctx = ExitStack()
    with ctx:
        def sb(name, shape, dt=fp32):
            return ctx.enter_context(nc.sbuf_tensor(name, shape, dt))

        def sem(name):
            return ctx.enter_context(nc.semaphore(name))

        arena = sb("arena", [P, 4 * DM])
        x_sb = arena[:, :].rearrange("p (t d) -> p t d", t=TILES)
        neglog = arena[:, 0:2 * DM].rearrange("p (b m n) -> p b m n", b=2, m=2)
        probs = arena[:, 2 * DM:4 * DM].rearrange("p (b m n) -> p b m n", b=2, m=2)
        area = sb("area", [P, 4 * DM])
        ht = area[:, :].bitcast(fp16).rearrange("p (h k s) -> p h k s", h=2, k=KT)
        y_sb = area[:, 2 * DM:4 * DM].rearrange("p (b d) -> p b d", b=2)
        stage = sb("stage", [P, 4, 2 * WIDTH])
        w_hi = sb("w_hi", [P, 3, KT, WIDTH], fp16)
        w_lo = sb("w_lo", [P, 3, KT, WIDTH], fp16)
        q_hi = sb("q_hi", [P, 2 * CHUNKS, SEQ], fp16)
        q_lo = sb("q_lo", [P, 2 * CHUNKS, SEQ], fp16)
        at_hi = q_hi[:, 0:CHUNKS, :].rearrange("p c (e s) -> p (c e) s", s=P).rearrange("p (b e) s -> p b e s", b=2)
        at_lo = q_lo[:, 0:CHUNKS, :].rearrange("p c (e s) -> p (c e) s", s=P).rearrange("p (b e) s -> p b e s", b=2)
        k_pair = sb("k_pair", [P, 2, 2 * CHUNKS, SEQ], fp16)
        v_hi = sb("v_hi", [P, TILES, 2 * WIDTH], fp16)
        v_lo = sb("v_lo", [P, TILES, 2 * WIDTH], fp16)
        gates = sb("gates", [P, 2, TILES, WIDTH])
        strips = sb("strips", [P, HEADS, SEQ])
        pt_hi = sb("pt_hi", [P, 2, 2, SEQ], fp16)
        pt_lo = sb("pt_lo", [P, 2, 2, SEQ], fp16)
        g_row = sb("g_row", [P, DM])
        subln = sb("subln", [P, 2 * DH])
        tanh_sb = strips[:, 0:2, :]
        q_twice = sb("q_twice", [P, 2, 2, CHUNKS, P], fp16)
        heads_out = sb("heads_out", [P, WIDTH])
        k_natural = gates[:, 1, 0:2, :].bitcast(fp16).rearrange("p b (h s) -> p b h s", h=2)
        junk = sb("junk", [P, DM], fp16)
        ident = sb("ident", [P, P])
        negmax = sb("negmax", [P, NSTEP, 2])
        sums = sb("sums", [P, NSTEP, 2])
        rsums = sb("rsums", [P, NSTEP, 2])
        ratio = sb("ratio", [P, HALF])
        lam_in = sb("lam_in", [P, 4, DH])
        lam_junk = sb("lam_junk", [P, 2, DH])
        lam_dot = sb("lam_dot", [P, 2])
        lam_exp = sb("lam_exp", [P, 2])
        neglam = sb("neglam", [P, 1])
        minus_half = sb("minus_half", [P, 4])
        x_sq = sb("x_sq", [P, TILES])
        x_ms = sb("x_ms", [P, TILES])
        x_rstd = sb("x_rstd", [P, TILES])
        sub_sq = sb("sub_sq", [P, TILES, DIFF_HEADS])
        sub_ms = sb("sub_ms", [P, TILES, DIFF_HEADS])
        sub_rstd = sb("sub_rstd", [P, TILES, DIFF_HEADS])
        y_sq = sb("y_sq", [P, TILES, 2])
        y_part = sb("y_part", [P, TILES])
        y_ms = sb("y_ms", [P, TILES])
        y_rstd = sb("y_rstd", [P, TILES])
        bias_area = q_twice[0:HEADS, :, :, :, :].rearrange("p b m c s -> p (b m c s)").bitcast(fp32)
        row_sb = bias_area[:, 0:ROW]
        rel_t = bias_area[:, ROW:ROW + BUCKETS]

        unit_ps = ctx.enter_context(nc.psum_tensor("unit_ps", [P, 2, 512], fp32))
        score_ps = ctx.enter_context(nc.psum_tensor("score_ps", [P, 2, 512], fp32))
        pt_ps = ctx.enter_context(nc.psum_tensor("pt_ps", [P, 2, 512], fp32))
        o_ps = ctx.enter_context(nc.psum_tensor("o_ps", [P, 2, 512], fp32))
        xt_banks = [pt_ps, score_ps]

        def x_part(t, part):
            n = KT // X_PARTS[t]
            banks = xt_banks[t % 2][:, part:part + 2 // X_PARTS[t], :]
            return (ht[:, :, part * n:(part + 1) * n, t * P:(t + 1) * P],
                    banks.rearrange("p b (k s) -> p (b k) s", s=P))

        x_loaded = [sem(f"x_loaded{t}") for t in range(TILES)]
        gpre_loaded = sem("gpre_loaded")
        gpost_loaded = sem("gpost_loaded")
        small_loaded = sem("small_loaded")
        rel_loaded = sem("rel_loaded")
        rows_stored = sem("rows_stored")
        strips_loaded = sem("strips_loaded")
        w_loaded = [sem(f"w_loaded{i}") for i in range(4)]
        xres_loaded = sem("xres_loaded")
        stored = [sem(f"stored{i}") for i in range(2)]
        stored_last = sem("stored_last")
        split_hi = sem("split_hi")
        split_lo = sem("split_lo")
        consts_ready = sem("consts_ready")
        ident_zero = sem("ident_zero")
        x_squared = sem("x_squared")
        x_mean = sem("x_mean")
        x_rstd_ready = sem("x_rstd_ready")
        xs_ready = sem("xs_ready")
        ht_hi_ready = sem("ht_hi_ready")
        ht_ready = sem("ht_ready")
        unit_done = sem("unit_done")
        unit_read = sem("unit_read")
        unit_freed = sem("unit_freed")
        q_doubled = sem("q_doubled")
        k_paired = sem("k_paired")
        row_built = sem("row_built")
        row_masked = sem("row_masked")
        lam_dots = sem("lam_dots")
        lam_exps = sem("lam_exps")
        lam_ready = sem("lam_ready")
        score_ready = sem("score_ready")
        logits_ready = sem("logits_ready")
        exp_done = sem("exp_done")
        rsum_ready = sem("rsum_ready")
        ratio_ready = sem("ratio_ready")
        combined = sem("combined")
        pt_ready = sem("pt_ready")
        pt_read = sem("pt_read")
        pt_freed = sem("pt_freed")
        values_done = sem("values_done")
        o_freed = sem("o_freed")
        sub_squared = sem("sub_squared")
        sub_mean = sem("sub_mean")
        sub_rstd_ready = sem("sub_rstd_ready")
        sub_scaled = sem("sub_scaled")
        gate_silu = sem("gate_silu")
        diff_gated = sem("diff_gated")
        gated = sem("gated")
        at_turned = sem("at_turned")
        at_read = sem("at_read")
        at_ready = sem("at_ready")
        y_weighted = sem("y_weighted")
        y_squared = sem("y_squared")
        y_part_ready = sem("y_part_ready")
        y_mean = sem("y_mean")
        y_rstd_ready = sem("y_rstd_ready")
        y_ready = sem("y_ready")
        diff_normed = sem("diff_normed")

        block = ctx.enter_context(nc.Block())

        @block.sync
        def _(sp):
            def load_quarter(n):
                if n >= 4:
                    sp.wait_ge(split_lo, n - 3)
                g, k = n // 4, 2 * (n % 4)
                if g < len(GROUPS):
                    col = GROUPS[g][2]
                    src = w_in_v[:, k:k + 2, col:col + WIDTH]
                else:
                    col = (g - len(GROUPS)) * WIDTH
                    src = w_out_v[:, k:k + 2, col:col + WIDTH]
                sp.dma_start(stage[:, n % 4, :].rearrange("p (k n) -> p k n", k=2), src)\
                    .then_inc(w_loaded[n % 4], 16)

            def double_queries(m):
                r, t, _ = STEPS[4 * m]
                if m:
                    sp.wait_ge(q_doubled, 64 * m)
                if m >= 2:
                    sp.wait_ge(score_ready, SCORE_USES_X + 4 * (m - 1))
                sp.wait_ge(unit_freed, UNIT["q", r, CHUNKS - 1] + 1)
                for head in range(2):
                    src = q_hi[head * DH:(head + 1) * DH, r * CHUNKS:(r + 1) * CHUNKS, t * P:(t + 1) * P]
                    for half in range(2):
                        sp.dma_start(q_twice[half * DH:(half + 1) * DH, m % 2, head, :, :], src)\
                            .then_inc(q_doubled, 16)

            def pair_keys(u):
                _, r, c, _ = unit_of(u)
                sp.wait_ge(unit_freed, u + 1)
                if K_UNITS.index(u):
                    sp.wait_ge(k_paired, 64 * K_UNITS.index(u))
                for head in range(2):
                    for part in range(2):
                        half = (head + part) % 2
                        sp.dma_start(k_pair[half * DH:(half + 1) * DH, head, r * CHUNKS + c, :],
                                     k_natural[head * DH:(head + 1) * DH, u % 2, part, :]).then_inc(k_paired, 16)

            def load_x(t):
                sp.dma_start(x_sb[:, t, :], x_v[t]).then_inc(x_loaded[t], 16)

            load_x(0)
            sp.dma_start(g_row[:, :], norm_pre_g[0].partition_broadcast(P)).then_inc(gpre_loaded, 16)
            load_quarter(0)
            load_quarter(1)
            load_x(1)
            load_quarter(2)
            load_quarter(3)
            load_x(2)
            load_x(3)
            with nc.allow_non_contiguous_dma(reason="32 x 12 table, transposed once"):
                sp.dma_start(rel_t, rel_bias.rearrange("b h -> h b")).then_inc(rel_loaded, 16)
            sp.dma_start(lam_in[:, :, :], diff_lambda[0].partition_broadcast(P)).then_inc(small_loaded, 16)
            sp.dma_start(subln[:, :], diff_subln_g[0].partition_broadcast(P)).then_inc(small_loaded, 16)
            for n in range(4, 8):
                load_quarter(n)
            sp.wait_ge(row_built, 1)
            sp.dma_start(bias_rows.ap(), row_sb).then_inc(rows_stored, 16)
            load_quarter(8)
            sp.wait_ge(rows_stored, 16)
            sp.dma_start(strips[:, :, :], strip_view).then_inc(strips_loaded, 16)
            sp.wait_ge(xs_ready, x_count(TILES - 1))
            sp.dma_start(g_row[:, :], norm_post_g[0].partition_broadcast(P)).then_inc(gpost_loaded, 16)
            for u in range(1, FIRST_UNITS):
                load_quarter(u + 8)
                if u == UNIT["q", 0, CHUNKS - 1]:
                    double_queries(0)
                if u in K_UNITS:
                    pair_keys(u)
            for j in range(SLOTS):
                if j in TWICE_SLOT:
                    double_queries(TWICE_SLOT[j])
                if FIRST_UNITS + 8 + j < QUARTERS:
                    load_quarter(FIRST_UNITS + 8 + j)
                for u in FILL_END[j]:
                    if u in K_UNITS:
                        pair_keys(u)
                if j == XRES_SLOT:
                    sp.wait_ge(split_lo, QUARTERS)
                    sp.dma_start(stage[:, :, :], x[0].rearrange("(t p) d -> p t d", p=P))\
                        .then_inc(xres_loaded, 16)
            for i, t in enumerate(DOWN[:-1]):
                sp.wait_ge(y_ready, i + 1)
                sp.dma_start(out_v[t], y_sb[:, t % 2, :]).then_inc(stored[t % 2], 16)
            for half in range(2):
                cols = slice(half * WIDTH, (half + 1) * WIDTH)
                sp.wait_ge(y_ready, TILES + half)
                sp.dma_start(out_v[0][:, cols], y_sb[:, 0, cols]).then_inc(stored_last, 16)
            sp.wait_ge(stored[0], 16)
            sp.wait_ge(stored[1], 16 * 2)
            sp.wait_ge(stored_last, 16 * 2)

        @block.gpsimd
        def _(pool):
            nc.gpsimd.memset(ident[:, :], 0.0).then_inc(ident_zero, 1)
            nc.gpsimd.memset(minus_half[:, :], -0.5).then_inc(consts_ready, 1)
            pool.wait_ge(ident_zero, 1)
            nc.gpsimd.affine_select(out=ident[:, :], in_=ident[:, :], compare_op=ALU.not_equal, fill=1.0,
                                    base=0, pattern=[[-1, P]], channel_multiplier=1).then_inc(consts_ready, 1)
            pool.wait_ge(consts_ready, 2)
            for t in range(TILES):
                pool.wait_ge(x_squared, t + 1)
                nc.gpsimd.tensor_scalar(x_ms[:, t:t + 1], x_sq[:, t:t + 1], NORM_EPS, 1.0,
                                        ALU.add, ALU.mult).then_inc(x_mean, 1)
                pool.wait_ge(x_mean, t + 1)
                nc.gpsimd.tensor_tensor(x_rstd[:, t:t + 1], x_ms[:, t:t + 1], minus_half[:, 0:1],
                                        ALU.pow).then_inc(x_rstd_ready, 1)
            nc.gpsimd.memset(row_sb[:, 0:P - 1], MASKED).then_inc(row_masked, 1)
            pool.wait_ge(rel_loaded, 16)
            for b in range(BUCKETS):
                lo = first_distance(b)
                hi = first_distance(b + 1) if b + 1 < BUCKETS else SEQ + 1
                last = nc.gpsimd.tensor_copy(row_sb[:, P - 1 + lo:P - 1 + hi],
                                             rel_t[:, b:b + 1].to_broadcast([HEADS, hi - lo]))
                if b == BUCKETS - 1:
                    last.then_inc(row_built, 1)
            pool.wait_ge(small_loaded, 32)
            keep = (1.0 - LAMBDA_INIT) ** 2
            for i, t in enumerate(DOWN):
                pool.wait_ge(sub_squared, DIFF_HEADS * (i + 1))
                nc.gpsimd.tensor_scalar(sub_ms[:, t, :], sub_sq[:, t, :], 1.0 / (2 * DH * keep),
                                        SUBLN_EPS / keep, ALU.mult, ALU.add).then_inc(sub_mean, 1)
                pool.wait_ge(sub_mean, i + 1)
                nc.gpsimd.tensor_tensor(sub_rstd[:, t, :], sub_ms[:, t, :], minus_half[:, :],
                                        ALU.pow).then_inc(sub_rstd_ready, 1)
                pool.wait_ge(sub_rstd_ready, i + 1)
                rows = gates[:, 0, t, :].rearrange("p (h d) -> p h d", h=DIFF_HEADS)
                nc.gpsimd.tensor_tensor(rows, rows, sub_rstd[:, t, :].unsqueeze(2).to_broadcast([P, DIFF_HEADS, P]),
                                        ALU.mult).then_inc(sub_scaled, 1)
                pool.wait_ge(sub_scaled, i + 1)
                nc.gpsimd.tensor_tensor(rows, rows, subln[:, :].unsqueeze(1).to_broadcast([P, DIFF_HEADS, P]),
                                        ALU.mult).then_inc(diff_normed, 1)
            for i, t in enumerate(DOWN):
                pool.wait_ge(y_squared, 2 * i + 1)
                nc.gpsimd.tensor_scalar(y_part[:, t:t + 1], y_sq[:, t, 0:1], NORM_EPS * W_SCALE ** 2, 1.0,
                                        ALU.add, ALU.mult).then_inc(y_part_ready, 1)
                pool.wait_ge(y_part_ready, i + 1)
                pool.wait_ge(y_squared, 2 * (i + 1))
                nc.gpsimd.tensor_tensor(y_ms[:, t:t + 1], y_sq[:, t, 1:2], y_part[:, t:t + 1],
                                        ALU.add).then_inc(y_mean, 1)
                pool.wait_ge(y_mean, i + 1)
                nc.gpsimd.tensor_tensor(y_rstd[:, t:t + 1], y_ms[:, t:t + 1], minus_half[:, 0:1],
                                        ALU.pow).then_inc(y_rstd_ready, 1)

        @block.tensor
        def _(pe):
            def x_transposes(t, part=0):
                pe.wait_ge(xs_ready, x_count(t, part))
                if t >= 2:
                    pe.wait_ge(ht_ready, x_count(t - 2, X_PARTS[t - 2] - 1))
                n = KT // X_PARTS[t]
                for k in range(part * n, (part + 1) * n):
                    last = nc.tensor.transpose(xt_banks[t % 2][:, k // 4, (k % 4) * P:(k % 4 + 1) * P],
                                               x_sb[:, t, k * P:(k + 1) * P], ident[:, :])
                last.then_inc(pt_ready if t % 2 == 0 else score_ready, 1)

            def warm_up(n):
                for _ in range(n):
                    nc.tensor.matmul(unit_ps[:, 1, 0:P], ident[:, :], ident[:, :], start=True, stop=True)

            def unit_quarter(u, q):
                kind, half, i, g = unit_of(u)
                bank = unit_ps[:, u % 2, :]
                if q == 0:
                    if u >= IN_UNITS + 2:
                        pe.wait_ge(y_weighted, u - 1 - IN_UNITS)
                    elif u >= 2:
                        pe.wait_ge(unit_freed, u - 1)
                    if kind == "y":
                        pe.wait_ge(at_ready, 2 * (TILES - i))
                    else:
                        pe.wait_ge(ht_ready, x_count(i if kind in "vg" else TILES - 1))
                if (u, q) == (0, 2):
                    pe.wait_ge(ht_ready, 2)
                pe.wait_ge(split_lo, 4 * g + q + 1)
                for k in (2 * q, 2 * q + 1):
                    wh, wl = w_hi[:, g % 3, k, :], w_lo[:, g % 3, k, :]
                    if kind in "qk":
                        cols = slice(i * P, (i + 1) * P)
                        terms = [(wh[:, cols], ht[:, 0, k, :]), (wh[:, cols], ht[:, 1, k, :]),
                                 (wl[:, cols], ht[:, 0, k, :])]
                    elif kind == "y":
                        ah, al = at_hi[:, i % 2, k, :], at_lo[:, i % 2, k, :]
                        terms = [(ah, wh), (ah, wl), (al, wh)]
                    else:
                        rows = slice(i * P, (i + 1) * P)
                        hh, hl = ht[:, 0, k, rows], ht[:, 1, k, rows]
                        terms = [(hh, wh), (hh, wl), (hl, wh)]
                    for n, (a, b) in enumerate(terms):
                        last = nc.tensor.matmul(bank, a, b, start=(k == 0 and n == 0),
                                                stop=(k == KT - 1 and n == 2))
                if q == 3:
                    last.then_inc(unit_done, 1)

            def scores(i):
                r, t, c = STEPS[i]
                ch, n = r * CHUNKS + c, (t + 1) * P
                pe.wait_ge(q_doubled, 64 * (i // 4 + 1))
                pe.wait_ge(unit_freed, UNIT["q", r, c] + 1)
                pe.wait_ge(k_paired, 64 * (K_UNITS.index(UNIT["k", r, c]) + 1))
                if i >= 1:
                    pe.wait_ge(logits_ready, 2 * i)
                rows = slice(t * P, (t + 1) * P)
                for m in range(2):
                    nc.tensor.matmul(score_ps[:, m, 0:n], q_twice[:, (i // 4) % 2, m, c, :],
                                     k_pair[:, m, ch, 0:n], start=True, stop=False)
                for m in range(2):
                    part = slice(m * DH, (m + 1) * DH)
                    last = nc.tensor.matmul(score_ps[:, m, 0:n], q_lo[part, ch, rows],
                                            k_pair[part, m, ch, 0:n], start=False, stop=True)
                last.then_inc(score_ready, 1)

            def p_transposes(i):
                r, t, c = STEPS[i]
                if r == 0:
                    pe.wait_ge(combined, i + 1)
                else:
                    pe.wait_ge(exp_done, 2 * (i + 1))
                if pt_use("p", i):
                    pe.wait_ge(pt_freed, pt_use("p", i))
                for m in range(1 + r):
                    for k in range(t + 1):
                        cols = slice(k * P, (k + 1) * P)
                        last = nc.tensor.transpose(pt_ps[:, m, cols], probs[:, i % 2, m, cols], ident[:, :])
                last.then_inc(pt_ready, 1)

            def values(i):
                r, t, c = STEPS[i]
                o = i // 4
                if i % 4 == 0 and o >= 2:
                    pe.wait_ge(o_freed, o - 1)
                pe.wait_ge(unit_freed, UNIT["v", r, t] + 1)
                pe.wait_ge(pt_freed, pt_use("p", i) + 1)
                width = 2 * DH // (1 + r)
                for m in range(1 + r):
                    col = c * P + m * width
                    src = slice(r * WIDTH + col, r * WIDTH + col + width)
                    for k in range(t + 1):
                        ks = slice(k * P, (k + 1) * P)
                        ph, pl = pt_hi[:, i % 2, m, ks], pt_lo[:, i % 2, m, ks]
                        for n, (a, b) in enumerate(((ph, v_hi), (ph, v_lo), (pl, v_hi))):
                            last = nc.tensor.matmul(o_ps[:, o % 2, col:col + width], a, b[:, k, src],
                                                    start=(k == 0 and n == 0), stop=(k == t and n == 2))
                last.then_inc(values_done, 1)

            def a_transposes(t, half):
                pe.wait_ge(gated, TILES - t)
                pe.wait_ge(diff_gated, TILES - t)
                n = AT_ORDER.index((t, half))
                if half and t:
                    pe.wait_ge(at_ready, n)
                for e in range(CHUNKS):
                    cols = slice(e * P, (e + 1) * P)
                    last = nc.tensor.transpose(o_ps[:, at_bank(t, half), cols], gates[:, half, t, cols],
                                               ident[:, :])
                last.then_inc(at_turned, 1)

            pe.wait_ge(consts_ready, 2)
            warm_up(WARM_UP[0])
            for part in range(X_PARTS[0]):
                x_transposes(0, part)
            warm_up(WARM_UP[1])
            for u in range(FIRST_UNITS):
                for q in range(4):
                    unit_quarter(u, q)
                    if (u, q) == (0, 1):
                        x_transposes(1)
                if u + 2 < TILES:
                    x_transposes(u + 2)
            for j in range(SLOTS):
                if j < NSTEP:
                    scores(j)
                for u, q in FILL[j][0]:
                    unit_quarter(u, q)
                if j in AT_HALF:
                    a_transposes(*AT_HALF[j])
                if j >= 2:
                    values(j - 2)
                if 1 <= j <= NSTEP:
                    p_transposes(j - 1)
                for u, q in FILL[j][1]:
                    unit_quarter(u, q)
            for half in range(2):
                a_transposes(0, half)
            for u, q in FILL_LAST:
                unit_quarter(u, q)

        @block.scalar
        def _(act):
            last_square = []

            def square(dst, src, done, count, scale=ROOT_MEAN):
                if last_square:
                    act.wait_ge(*last_square.pop())
                n = src.shape[-1]
                nc.scalar.activation(junk[:, 0:n], src, ACT.Square, scale=scale, accum_out=dst).then_inc(done, 1)
                last_square.append((done, count))

            def split(n):
                g, k = n // 4, 2 * (n % 4)
                act.wait_ge(w_loaded[n % 4], 16 * (n // 4 + 1))
                if g >= 3:
                    act.wait_ge(unit_done, 4 * (g - 2))
                nc.scalar.activation(w_hi[:, g % 3, k:k + 2, :],
                                     stage[:, n % 4, :].rearrange("p (k n) -> p k n", k=2),
                                     ACT.Copy, scale=W_SCALE).then_inc(split_hi, 1)

            def unit(u):
                kind, r, i, g = unit_of(u)
                act.wait_ge(unit_done, u + 1)
                if kind == "y":
                    square(y_sq[:, i, r:r + 1], unit_ps[:, u % 2, :], y_squared, u - IN_UNITS + 1)
                    return
                src = unit_ps[:, u % 2, :]
                if kind == "g":
                    act.wait_ge(unit_freed, u - 1)
                    act.wait_ge(logits_ready, NSTEP)
                    if r == 0 and TILES - 1 - i >= 2:
                        act.wait_ge(diff_gated, TILES - 2 - i)
                    ins = nc.scalar.activation(tanh_sb[:, u % 2, :], src, ACT.Tanh, scale=0.5 * U_SCALE)
                elif kind == "v":
                    ins = nc.scalar.activation(v_hi[:, i, r * WIDTH:(r + 1) * WIDTH], src, ACT.Copy,
                                               scale=U_SCALE)
                elif kind == "q":
                    ins = nc.scalar.activation(q_hi[:, r * CHUNKS + i, :], src, ACT.Copy, scale=Q_SCALE)
                else:
                    if K_UNITS.index(u) >= 2:
                        act.wait_ge(k_paired, 64 * (K_UNITS.index(u) - 1))
                    ins = nc.scalar.activation(k_natural[:, u % 2, 0, :], src, ACT.Copy, scale=U_SCALE)
                ins.then_inc(unit_read, 1)

            def x_hi(t, part=0):
                if t % 2 == 0:
                    act.wait_ge(pt_ready, PT_USE["x", t, part] + 1)
                else:
                    act.wait_ge(score_ready, t // 2 + 1)
                dst, src = x_part(t, part)
                nc.scalar.activation(dst[:, 0], src, ACT.Copy).then_inc(ht_hi_ready, 1)

            def exps(i):
                r, t, c = STEPS[i]
                n = (t + 1) * P
                if i >= 2:
                    act.wait_ge(pt_ready, PT_USE["p", i - 2] + 1)
                for m in range(2):
                    act.wait_ge(logits_ready, 2 * i + m + 1)
                    nc.scalar.activation(probs[:, i % 2, m, 0:n], neglog[:, i % 2, m, 0:n], ACT.Exp,
                                         bias=negmax[:, i, m:m + 1], scale=-1.0,
                                         accum_out=sums[:, i, m:m + 1]).then_inc(exp_done, 1)

            def p_hi(i):
                r, t, c = STEPS[i]
                n = (t + 1) * P
                if i >= 2:
                    act.wait_ge(values_done, i - 1)
                act.wait_ge(pt_ready, PT_USE["p", i] + 1)
                nc.scalar.activation(pt_hi[:, i % 2, 0:1 + r, 0:n], pt_ps[:, 0:1 + r, 0:n],
                                     ACT.Copy).then_inc(pt_read, 1)

            def a_hi(t, half):
                n = AT_ORDER.index((t, half))
                act.wait_ge(at_turned, n + 1)
                if t < 2:
                    act.wait_ge(unit_done, UNIT["y", 1, t + 2] + 1)
                nc.scalar.activation(at_hi[:, t % 2, half * CHUNKS:(half + 1) * CHUNKS, :],
                                     o_ps[:, at_bank(t, half), :].rearrange("p (e s) -> p e s", s=P),
                                     ACT.Copy, scale=1.0 / GATE_SCALE).then_inc(at_read, 1)

            def x_square(t):
                act.wait_ge(x_loaded[t], 16)
                square(x_sq[:, t:t + 1], x_sb[:, t, :], x_squared, t + 1)

            x_square(0)
            split(0)
            x_hi(0, 0)
            x_hi(0, 1)
            split(1)
            x_square(1)
            split(2)
            split(3)
            x_square(2)
            x_hi(1)
            x_square(3)
            for u in range(FIRST_UNITS):
                if u + 2 < TILES:
                    x_hi(u + 2)
                split(u + SPLIT_AHEAD)
                unit(u)
                if u == 2:
                    act.wait_ge(lam_dots, 2)
                    nc.scalar.activation(lam_exp[:, :], lam_dot[:, :], ACT.Exp).then_inc(lam_exps, 1)
            for j in range(SLOTS):
                if j < NSTEP:
                    exps(j)
                if j in AT_HALF:
                    a_hi(*AT_HALF[j])
                if j >= 1 and j <= NSTEP:
                    p_hi(j - 1)
                for n in SPLIT_IN_SLOT[j]:
                    split(n)
                for u in FILL_END[j]:
                    unit(u)
                for (r, t), s in POST_SLOT.items():
                    if s == j and r == 0:
                        act.wait_ge(o_freed, TILES - t)
                        for h in range(DIFF_HEADS):
                            square(sub_sq[:, t, h:h + 1], gates[:, 0, t, h * P:(h + 1) * P], sub_squared,
                                   DIFF_HEADS * (TILES - 1 - t) + h + 1, scale=1.0)
            for half in range(2):
                a_hi(0, half)
            for u in LAST_UNITS:
                unit(u)

        @block.vector
        def _(dve):
            def split(n):
                g, k = n // 4, 2 * (n % 4)
                dve.wait_ge(split_hi, n + 1)
                nc.vector.scalar_tensor_tensor(w_lo[:, g % 3, k:k + 2, :],
                                               stage[:, n % 4, :].rearrange("p (k n) -> p k n", k=2), W_SCALE,
                                               w_hi[:, g % 3, k:k + 2, :], ALU.mult,
                                               ALU.subtract).then_inc(split_lo, 1)

            def unit(u):
                kind, r, i, g = unit_of(u)
                src = unit_ps[:, u % 2, :]
                if kind == "y":
                    dve.wait_ge(y_squared, u - IN_UNITS + 1)
                    if u == IN_UNITS:
                        dve.wait_ge(gpost_loaded, 16)
                    if i < 2:
                        dve.wait_ge(stored[i % 2], 16)
                    cols = slice(r * WIDTH, (r + 1) * WIDTH)
                    nc.vector.tensor_tensor(y_sb[:, i % 2, cols], src, g_row[:, cols], ALU.mult)\
                        .then_inc(y_weighted, 1)
                    return
                dve.wait_ge(unit_read, u + 1)
                if kind == "g" and r == 0:
                    nc.vector.scalar_tensor_tensor(tanh_sb[:, u % 2, :], tanh_sb[:, u % 2, :], 1.0, src,
                                                   ALU.add, ALU.mult).then_inc(unit_freed, 1)
                    dve.wait_ge(unit_freed, u + 1)
                    dve.wait_ge(diff_normed, TILES - i)
                    nc.vector.tensor_tensor(gates[:, 0, i, :], gates[:, 0, i, :], tanh_sb[:, u % 2, :],
                                            ALU.mult).then_inc(diff_gated, 1)
                    return
                if kind == "g":
                    dve.wait_ge(k_paired, 64 * len(K_UNITS))
                    ins = nc.vector.scalar_tensor_tensor(gates[:, r, i, :], tanh_sb[:, u % 2, :], 1.0, src,
                                                         ALU.add, ALU.mult)
                else:
                    if kind == "v":
                        hi, lo = (a[:, i, r * WIDTH:(r + 1) * WIDTH] for a in (v_hi, v_lo))
                    elif kind == "q":
                        hi, lo = (a[:, r * CHUNKS + i, :] for a in (q_hi, q_lo))
                    else:
                        hi, lo = k_natural[:, u % 2, 0, :], k_natural[:, u % 2, 1, :]
                    ins = nc.vector.scalar_tensor_tensor(lo, src, Q_SCALE if kind == "q" else U_SCALE, hi,
                                                         ALU.mult, ALU.subtract)
                ins.then_inc(unit_freed, 1)

            def x_norm(t, part=0):
                dve.wait_ge(x_rstd_ready, t + 1)
                if t == 0:
                    dve.wait_ge(gpre_loaded, 16)
                n = DM // X_PARTS[t]
                cols = slice(part * n, (part + 1) * n)
                nc.vector.scalar_tensor_tensor(x_sb[:, t, cols], x_sb[:, t, cols], x_rstd[:, t:t + 1],
                                               g_row[:, cols], ALU.mult, ALU.mult).then_inc(xs_ready, 1)

            def x_lo(t, part=0):
                dve.wait_ge(ht_hi_ready, x_count(t, part))
                dst, src = x_part(t, part)
                nc.vector.tensor_tensor(dst[:, 1], src, dst[:, 0], ALU.subtract).then_inc(ht_ready, 1)

            def logits(i):
                r, t, c = STEPS[i]
                n = (t + 1) * P
                if i >= 2:
                    dve.wait_ge(exp_done, 2 * (i - 1))
                dve.wait_ge(score_ready, SCORE_USES_X + i + 1)
                for m in range(2):
                    h = c if r == 0 else DIFF_HEADS + 2 * c + m
                    nc.vector.tensor_tensor_reduce(out=neglog[:, i % 2, m, 0:n], in0=score_ps[:, m, 0:n],
                                                   in1=strips[:, h, 0:n][:, ::-1], scale=-1.0, scalar=-MASKED,
                                                   op0=ALU.add, op1=ALU.min,
                                                   accum_out=negmax[:, i, m:m + 1]).then_inc(logits_ready, 1)

            def normalizers(i):
                r, t, c = STEPS[i]
                n = (t + 1) * P
                dve.wait_ge(exp_done, 2 * (i + 1))
                nc.vector.reciprocal(rsums[:, i, :], sums[:, i, :]).then_inc(rsum_ready, 1)
                if r == 0:
                    dve.wait_ge(rsum_ready, i + 1)
                    if i == 0:
                        dve.wait_ge(lam_ready, 1)
                    nc.vector.scalar_tensor_tensor(ratio[:, i:i + 1], rsums[:, i, 1:2], neglam[:, :],
                                                   sums[:, i, 0:1], ALU.mult, ALU.mult).then_inc(ratio_ready, 1)
                    dve.wait_ge(ratio_ready, i + 1)
                    p0, p1 = probs[:, i % 2, 0, 0:n], probs[:, i % 2, 1, 0:n]
                    nc.vector.scalar_tensor_tensor(p0, p1, ratio[:, i:i + 1], p0, ALU.mult,
                                                   ALU.add).then_inc(combined, 1)

            def p_lo(i):
                r, t, c = STEPS[i]
                n = (t + 1) * P
                dve.wait_ge(pt_read, pt_use("p", i) + 1)
                nc.vector.tensor_tensor(pt_lo[:, i % 2, 0:1 + r, 0:n], pt_ps[:, 0:1 + r, 0:n],
                                        pt_hi[:, i % 2, 0:1 + r, 0:n], ALU.subtract).then_inc(pt_freed, 1)

            def a_lo(t, half):
                dve.wait_ge(at_read, AT_ORDER.index((t, half)) + 1)
                chunks = slice(half * CHUNKS, (half + 1) * CHUNKS)
                nc.vector.scalar_tensor_tensor(
                    at_lo[:, t % 2, chunks, :].rearrange("p e s -> p (e s)"), o_ps[:, at_bank(t, half), :],
                    1.0 / GATE_SCALE, at_hi[:, t % 2, chunks, :].rearrange("p e s -> p (e s)"), ALU.mult,
                    ALU.subtract).then_inc(at_ready, 1)

            def head_rows(r, t, dst):
                i0 = r * HALF + 4 * (TILES - 1 - t)
                o = i0 // 4
                dve.wait_ge(values_done, i0 + 4)
                dve.wait_ge(rsum_ready, i0 + 4)
                heads = DIFF_HEADS * (1 + r)
                f = rsums[:, i0:i0 + 4, 0] if r == 0 else rsums[:, i0:i0 + 4, :].rearrange("p i m -> p (i m)")
                nc.vector.tensor_tensor(dst.rearrange("p (h d) -> p h d", h=heads),
                                        o_ps[:, o % 2, :].rearrange("p (h d) -> p h d", h=heads),
                                        f.unsqueeze(2).to_broadcast([P, heads, WIDTH // heads]),
                                        ALU.mult).then_inc(o_freed, 1)

            def gate_moba(t):
                i = TILES - 1 - t
                if i:
                    dve.wait_ge(gated, i)
                head_rows(1, t, heads_out[:, :])
                dve.wait_ge(o_freed, TILES + i + 1)
                nc.vector.tensor_tensor(gates[:, 1, t, :], heads_out[:, :], gates[:, 1, t, :],
                                        ALU.mult).then_inc(gated, 1)

            def finish_rows(t):
                i = TILES - 1 - t
                parts = 1 if t else 2
                dve.wait_ge(y_weighted, 2 * (i + 1))
                dve.wait_ge(y_rstd_ready, i + 1)
                if i == 0:
                    dve.wait_ge(xres_loaded, 16)
                for part in range(parts):
                    cols = slice(part * DM // parts, (part + 1) * DM // parts)
                    nc.vector.scalar_tensor_tensor(y_sb[:, t % 2, cols], y_sb[:, t % 2, cols],
                                                   y_rstd[:, t:t + 1], stage[:, t, cols], ALU.mult,
                                                   ALU.add).then_inc(y_ready, 1)

            x_norm(0, 0)
            x_norm(0, 1)
            split(0)
            x_lo(0, 0)
            x_lo(0, 1)
            split(1)
            x_norm(1)
            split(2)
            split(3)
            x_norm(2)
            x_lo(1)
            x_norm(3)
            dve.wait_ge(small_loaded, 32)
            for i in range(2):
                nc.vector.tensor_tensor_reduce(out=lam_junk[:, i, :], in0=lam_in[:, 2 * i, :],
                                               in1=lam_in[:, 2 * i + 1, :], scale=1.0, scalar=0.0,
                                               op0=ALU.mult, op1=ALU.add,
                                               accum_out=lam_dot[:, i:i + 1]).then_inc(lam_dots, 1)
            for u in range(FIRST_UNITS):
                if u + 2 < TILES:
                    x_lo(u + 2)
                split(u + SPLIT_AHEAD)
                unit(u)
                if u == 2:
                    dve.wait_ge(lam_exps, 1)
                    nc.vector.scalar_tensor_tensor(neglam[:, :], lam_exp[:, 1:2], -LAMBDA_INIT,
                                                   lam_exp[:, 0:1], ALU.add, ALU.subtract)\
                        .then_inc(lam_ready, 1)
            dve.wait_ge(strips_loaded, 16)
            for j in range(SLOTS):
                if j < NSTEP:
                    logits(j)
                if j in AT_HALF:
                    a_lo(*AT_HALF[j])
                if j >= 1 and j <= NSTEP:
                    p_lo(j - 1)
                if j < NSTEP:
                    normalizers(j)
                for (r, t), s in POST_SLOT.items():
                    if s == j and r == 1:
                        gate_moba(t)
                for t in DOWN[:-1]:
                    if UNIT["y", 1, t] in (FILL_END[j - 1] if j else []):
                        finish_rows(t)
                for n in SPLIT_IN_SLOT[j]:
                    split(n)
                for u in FILL_END[j]:
                    unit(u)
                for (r, t), s in POST_SLOT.items():
                    if s == j and r == 0:
                        head_rows(0, t, gates[:, 0, t, :])
            for half in range(2):
                a_lo(0, half)
            for u in LAST_UNITS:
                unit(u)
                if UNIT["y", 1, 1] == u - 1:
                    finish_rows(1)
            finish_rows(0)


_INS = ["x", "norm_pre_g", "w_in", "diff_lambda", "diff_subln_g", "w_out", "norm_post_g", "rel_bias"]


def kernel(**inputs):
    import numpy as _np
    import concourse.bacc as _bacc
    from concourse import mybir as _mybir
    from concourse.bass_utils import run_bass_kernel_spmd as _run

    nc = _bacc.Bacc("TRN2", target_bir_lowering=False, num_devices=1)
    arrays, args = {}, []
    for name in _INS:
        a = _np.ascontiguousarray(inputs[name])
        arrays[f"in_{name}_dram"] = a
        args.append(nc.dram_tensor(f"in_{name}_dram", a.shape, _mybir.dt.from_np(a.dtype),
                                   kind="ExternalInput").ap())
    shape = arrays["in_x_dram"].shape
    args.append(nc.dram_tensor("out_dram", shape, _mybir.dt.float32, kind="ExternalOutput").ap())
    bass_hymba_diff_moba_layer(nc, *args)
    r = _run(nc, [arrays], core_ids=[0])
    return r.results[0]["out_dram"]
```
